# Optimizing a Trainium2 kernel written in Bass

```python
import jax, jax.numpy as jnp
from jax import lax
import numpy as np

D_MODEL = 1024
BATCH = 1
SEQ = 512
DEPTH = 1
DEC_BATCH = 8
DEC_SEQ = 16
PAST_LEN = 256

CHUNK = 64
D_A = 512
A_GROUPS = 4
A_GROUP_DIM = D_A // A_GROUPS
GMLP_CHUNK = 128
D_B = 512
B_HEADS = 8
B_HEAD_DIM = D_B // B_HEADS
CONV_WIDTH = 4
LRU_C = 8.0
D_IN = 2 * D_A + 2 * D_B
D_MIX = D_A + D_B
PEER_HEADS = 8
N_KEYS = 128
N_EXPERTS = N_KEYS * N_KEYS
D_KEY = 256
D_HALF = D_KEY // 2
PEER_TOPK = 16
PEER_BLOCK = 128
EPS = 1e-6

kernel_name = "hybrid_gmlp_rglru_peer_stream_step"

def rmsnorm(x, g):
    xf = x.astype(jnp.float32)
    y = xf * lax.rsqrt(jnp.mean(xf * xf, axis=-1, keepdims=True) + EPS) * g.astype(jnp.float32)
    return y.astype(x.dtype)

def gmlp_mix(z, g_v, w_s, b_s):
    u, v = jnp.split(z, 2, axis=-1)
    v = rmsnorm(v, g_v)
    bsz, t, _ = v.shape
    L = min(t, GMLP_CHUNK)
    n = t // L
    vc = v.reshape(bsz, n, L, A_GROUPS, A_GROUP_DIM)
    mask = jnp.tril(jnp.ones((L, L), dtype=w_s.dtype))
    w = w_s[:, :L, :L] * mask
    s = jnp.einsum("gnm,bcmgd->bcngd", w, vc) + jnp.transpose(b_s[:, :L])[None, None, :, :, None]
    return u * s.reshape(bsz, t, D_A), v

def causal_conv(xb, buf, w, b):
    t = xb.shape[1]
    xp = jnp.concatenate([buf.astype(xb.dtype), xb], axis=1)
    y = b + xp[:, 0:t] * w[0]
    for k in range(1, CONV_WIDTH):
        y = y + xp[:, k:k + t] * w[k]
    return y, xp[:, -(CONV_WIDTH - 1):]

def _lin_combine(left, right):
    a1, b1 = left
    a2, b2 = right
    return a1 * a2, a2 * b1 + b2

def rg_lru(xc, h0, w_a, b_a, w_i, b_i, lam):
    bsz, t, _ = xc.shape
    xh = xc.reshape(bsz, t, B_HEADS, B_HEAD_DIM)
    r = jax.nn.sigmoid(jnp.einsum("bthi,hij->bthj", xh, w_a).reshape(bsz, t, D_B) + b_a)
    i = jax.nn.sigmoid(jnp.einsum("bthi,hij->bthj", xh, w_i).reshape(bsz, t, D_B) + b_i)
    log_a = LRU_C * r.astype(jnp.float32) * jax.nn.log_sigmoid(lam.astype(jnp.float32))
    a = jnp.exp(log_a)
    bx = jnp.sqrt(-jnp.expm1(2.0 * log_a)) * (i * xc).astype(jnp.float32)
    a_cum, b_cum = lax.associative_scan(_lin_combine, (a, bx), axis=1)
    h = a_cum * h0.astype(jnp.float32)[:, None, :] + b_cum
    return h.astype(xc.dtype), h[:, -1].astype(h0.dtype)

def peer(h, w_q, k1, k2, u_tab, v_tab):
    bsz, t, d = h.shape
    n = bsz * t
    nb = -(-n // PEER_BLOCK)
    xt = jnp.pad(h.reshape(n, d), ((0, nb * PEER_BLOCK - n), (0, 0))).reshape(nb, PEER_BLOCK, d)

    def block(xb):
        q = (xb @ w_q).reshape(PEER_BLOCK, PEER_HEADS, 2, D_HALF)
        s1 = jnp.einsum("thd,kd->thk", q[:, :, 0], k1).astype(jnp.float32)
        s2 = jnp.einsum("thd,kd->thk", q[:, :, 1], k2).astype(jnp.float32)
        v1, i1 = lax.top_k(s1, PEER_TOPK)
        v2, i2 = lax.top_k(s2, PEER_TOPK)
        cand = (v1[..., :, None] + v2[..., None, :]).reshape(PEER_BLOCK, PEER_HEADS, PEER_TOPK * PEER_TOPK)
        cidx = (i1[..., :, None] * N_KEYS + i2[..., None, :]).reshape(PEER_BLOCK, PEER_HEADS, PEER_TOPK * PEER_TOPK)
        top_s, sel = lax.top_k(cand, PEER_TOPK)
        eidx = jnp.take_along_axis(cidx, sel, axis=-1)
        g = jax.nn.softmax(top_s, axis=-1)
        u = u_tab[eidx]
        act = jax.nn.gelu(jnp.einsum("thkd,td->thk", u, xb).astype(jnp.float32))
        coef = (g * act).astype(xb.dtype)
        return jnp.einsum("thk,thkd->td", coef, v_tab[eidx])

    out = lax.map(block, xt).reshape(nb * PEER_BLOCK, d)[:n]
    return out.reshape(bsz, t, d)

def layer(x, conv_buf, h0, g_mix, w_in, g_v, w_s, b_s, conv_w, conv_b, w_a, b_a, w_i, b_i, lam,
          g_out_a, g_out_b, w_out, g_ffn, w_q, k1, k2, u_tab, v_tab):
    h = rmsnorm(x, g_mix)
    z = h @ w_in
    za = z[..., :2 * D_A]
    xb = z[..., 2 * D_A:2 * D_A + D_B]
    gate = z[..., 2 * D_A + D_B:]
    ya, v_rows = gmlp_mix(jax.nn.gelu(za), g_v, w_s, b_s)
    xc, new_buf = causal_conv(xb, conv_buf, conv_w, conv_b)
    yb, h_last = rg_lru(xc, h0, w_a, b_a, w_i, b_i, lam)
    yb = yb * jax.nn.gelu(gate)
    mix = jnp.concatenate([rmsnorm(ya, g_out_a), rmsnorm(yb, g_out_b)], axis=-1) @ w_out
    x = x + mix
    x = x + peer(rmsnorm(x, g_ffn), w_q, k1, k2, u_tab, v_tab)
    return x, new_buf, h_last, v_rows

def setup_inputs(seed: int = 0) -> dict:
    key = jax.random.key(seed)
    ks = jax.random.split(key, 32)
    f32 = jnp.float32
    nrm = lambda k, shape, s: jax.random.normal(k, shape, f32) * s
    gain = lambda k, shape: 1.0 + 0.01 * jax.random.normal(k, shape, f32)
    a0 = jax.random.uniform(ks[13], (DEPTH, D_B), f32, 0.9, 0.999) ** (1.0 / LRU_C)
    lam = jnp.log(a0) - jnp.log1p(-a0)
    return {
        "x_prompt": jax.random.normal(ks[0], (BATCH, SEQ, D_MODEL), f32),
        "x_sample": jax.random.normal(ks[1], (DEC_BATCH, DEC_SEQ, D_MODEL), f32),
        "state_conv": jax.random.normal(ks[2], (DEPTH, DEC_BATCH, CONV_WIDTH - 1, D_B), f32),
        "state_lru": 0.5 * jax.random.normal(ks[3], (DEPTH, DEC_BATCH, D_B), f32),
        "g_mix": gain(ks[4], (DEPTH, D_MODEL)),
        "w_in": nrm(ks[5], (DEPTH, D_MODEL, D_IN), D_MODEL ** -0.5),
        "g_v": gain(ks[6], (DEPTH, D_A)),
        "w_s": nrm(ks[7], (DEPTH, A_GROUPS, GMLP_CHUNK, GMLP_CHUNK), GMLP_CHUNK ** -0.5),
        "b_s": 1.0 + 0.1 * jax.random.normal(ks[8], (DEPTH, A_GROUPS, GMLP_CHUNK), f32),
        "conv_w": nrm(ks[9], (DEPTH, CONV_WIDTH, D_B), CONV_WIDTH ** -0.5),
        "conv_b": nrm(ks[10], (DEPTH, D_B), 0.02),
        "w_a": nrm(ks[11], (DEPTH, B_HEADS, B_HEAD_DIM, B_HEAD_DIM), B_HEAD_DIM ** -0.5),
        "b_a": nrm(ks[12], (DEPTH, D_B), 0.02),
        "w_i": nrm(ks[14], (DEPTH, B_HEADS, B_HEAD_DIM, B_HEAD_DIM), B_HEAD_DIM ** -0.5),
        "b_i": nrm(ks[15], (DEPTH, D_B), 0.02),
        "lam": lam,
        "g_out_a": gain(ks[16], (DEPTH, D_A)),
        "g_out_b": gain(ks[17], (DEPTH, D_B)),
        "w_out": nrm(ks[18], (DEPTH, D_MIX, D_MODEL), D_MIX ** -0.5),
        "g_ffn": gain(ks[19], (DEPTH, D_MODEL)),
        "w_q": nrm(ks[20], (DEPTH, D_MODEL, PEER_HEADS * D_KEY), D_MODEL ** -0.5),
        "k_sub1": nrm(ks[21], (DEPTH, N_KEYS, D_HALF), D_HALF ** -0.5),
        "k_sub2": nrm(ks[22], (DEPTH, N_KEYS, D_HALF), D_HALF ** -0.5),
        "u_tab": nrm(ks[23], (DEPTH, N_EXPERTS, D_MODEL), D_MODEL ** -0.5),
        "v_tab": nrm(ks[24], (DEPTH, N_EXPERTS, D_MODEL), PEER_HEADS ** -0.5),
        "g_final": gain(ks[25], (D_MODEL,)),
    }

def reference(x_prompt, x_sample, state_conv, state_lru, g_mix, w_in, g_v, w_s, b_s, conv_w, conv_b,
              w_a, b_a, w_i, b_i, lam, g_out_a, g_out_b, w_out, g_ffn, w_q, k_sub1, k_sub2,
              u_tab, v_tab, g_final):
    xp = x_prompt
    xs = x_sample
    conv_p, lru_p, conv_s, lru_s, vrows_s = [], [], [], [], []
    for l in range(DEPTH):
        p = (g_mix[l], w_in[l], g_v[l], w_s[l], b_s[l], conv_w[l], conv_b[l], w_a[l], b_a[l],
             w_i[l], b_i[l], lam[l], g_out_a[l], g_out_b[l], w_out[l], g_ffn[l], w_q[l],
             k_sub1[l], k_sub2[l], u_tab[l], v_tab[l])
        buf0 = jnp.zeros((xp.shape[0], CONV_WIDTH - 1, D_B), xp.dtype)
        h00 = jnp.zeros((xp.shape[0], D_B), xp.dtype)
        xp, cb, hl, _ = layer(xp, buf0, h00, *p)
        conv_p.append(cb)
        lru_p.append(hl)
        xs, cb, hl, vr = layer(xs, state_conv[l], state_lru[l], *p)
        conv_s.append(cb)
        lru_s.append(hl)
        vrows_s.append(vr)
    y_prompt = rmsnorm(xp, g_final)
    y_sample = rmsnorm(xs, g_final)
    new_conv_prompt = jnp.stack(conv_p)
    new_lru_prompt = jnp.stack(lru_p)
    new_conv_sample = jnp.stack(conv_s)
    new_lru_sample = jnp.stack(lru_s)
    new_gmlp_v_sample = jnp.stack(vrows_s)
    return (y_prompt, y_sample, new_conv_prompt, new_lru_prompt, new_conv_sample, new_lru_sample, new_gmlp_v_sample)


_drawn_inputs = setup_inputs


def setup_inputs(seed=0):
    import zlib

    import numpy as np

    out = dict(_drawn_inputs(seed))
    spreads = {}
    factors = {'g_mix': 10.779,
     'g_v': 30.24,
     'b_a': 7.835,
     'b_i': 6.561,
     'g_out_a': 30.649,
     'g_out_b': 31.888,
     'g_ffn': 25.224,
     'g_final': 174.883,
     'conv_b': 3.157}
    for name, (base, spread) in spreads.items():
        noise = np.random.default_rng([zlib.crc32(name.encode()), seed]).standard_normal(out[name].shape)
        drawn = base * np.exp(spread * noise) if base else spread * noise
        out[name] = __import__('jax').numpy.asarray(drawn.astype(out[name].dtype))
    for name, factor in factors.items():
        out[name] = (out[name] * factor).astype(out[name].dtype)
    return out
```

```python
from contextlib import ExitStack

import concourse.bass as bass
from concourse import mybir

F32 = mybir.dt.float32
I32 = mybir.dt.int32
U32 = mybir.dt.uint32
ALU = mybir.AluOpType
ACT = mybir.ActivationFunctionType
AX_X = mybir.AxisListType.X

P = 128
D = 1024
DC = D // P
DH = 512
HC = DH // P
GROUPS = 4
TILES = 5
NB, NT = 8, 16
TAPS = 4
HIST = TAPS - 1
SEGS = NT + HIST
HEADS = 8
TOPK = 16
SLOTS = HEADS * TOPK
RING = 6
PAIRS = SLOTS // 2
DIAGS = 4
PIECES = 6
NORMS = 9
EPS = 1e-6
LOWEST = -3.0e38
LRU_C = 8.0

COLS = {}
_at = 0
for _name, _n in (("g_mix", DC), ("g_a", HC), ("g_b", HC), ("conv_w", HC * TAPS), ("conv_b", HC), ("b_a", HC),
                  ("b_i", HC), ("lam", HC), ("bs_prompt", GROUPS), ("bs_sample", GROUPS)):
    COLS[_name] = (_at, _at + _n)
    _at += _n
NCOLS = _at


class When:

    def __init__(self, offset, reg=None):
        self.offset, self.reg = offset, reg

    def __call__(self, per, k):
        fixed = self.offset * per + k
        return fixed if self.reg is None else self.reg * per + fixed


class Steps:

    def __init__(self, eng, own, held):
        self.eng, self.own, self.held = eng, own, held
        self.per, self.count, self.last = 0, 0, None

    def after(self):
        if self.last is not None:
            self.eng.wait_ge(*self.last)

    def after_held(self):
        self.after()
        self.eng.sem_inc(self.held, 1)

    def step(self, ins, n):
        self.count += 1
        ins.then_inc(self.own, 1)
        self.last = (self.own, n(self.per, self.count))

    def gives(self, ins, sem, value):
        ins.then_inc(sem, 1)
        self.last = (sem, value)


def hybrid_layer(nc, x_all, cols, conv_state, lru_state, w_in, w_out, w_q, ws_t, w_a, w_i, keys_t, rows, experts,
                 y_all, v_rows, state_sample, state_prompt):
    with ExitStack() as ctx:
        def sb(name, shape, dt=F32):
            return ctx.enter_context(nc.sbuf_tensor(name, [P] + shape, dt))

        def sem(name):
            return ctx.enter_context(nc.semaphore(name))

        ring = sb("ring", [RING, 2 * D])
        wbuf = sb("wbuf", [2, DC, 512])
        wq = sb("wq", [DC, 2 * SLOTS * TOPK // 2])
        xn = sb("xn", [D])
        h2n = sb("h2n", [D])
        x1 = sb("x1", [D])
        h2 = sb("h2", [D])
        hT = sb("hT", [DC, P])
        tmpA = sb("tmpA", [D])
        tmpB = sb("tmpB", [D])
        ug = sb("ug", [DH])
        vg = sb("vg", [DH])
        gg = sb("gg", [HC, P])
        xbuf = sb("xbuf", [HC, NB * SEGS])
        xc = sb("xc", [HC, P])
        hl = ug[:].rearrange("p (m t) -> p m t", m=HC)
        g_ffn = sb("g_ffn", [D])
        g_fin = sb("g_fin", [D])
        g_v = sb("g_v", [DH])
        ws = sb("ws", [GROUPS, P])
        wab = sb("wab", [HC, P])
        wib = sb("wib", [HC, P])
        keys = sb("keys", [2, P])
        ident = sb("ident", [P])
        ones = sb("ones", [2])
        iota_i = sb("iota_i", [TOPK], I32)
        iota = sb("iota", [TOPK])
        par = sb("par", [NCOLS])
        nbias = sb("nbias", [2 * HC])
        lamc = sb("lamc", [HC])
        lt = sb("lt", [6, HC])
        carry = sb("carry", [HC, NB])
        cin = sb("cin", [HC, NB])
        last = sb("last", [HC, NB * (HIST + 1)])
        ssq = sb("ssq", [8])
        rms = sb("rms", [8])
        rs = sb("rs", [8])
        eps = sb("eps", [1])
        yrms = sb("yrms", [4])
        vals = sb("vals", [2, TOPK])
        idx8 = sb("idx8", [2, TOPK], U32)
        idxf = sb("idxf", [2, TOPK])
        best = sb("best", [HEADS, TOPK])
        sel = sb("sel", [TOPK], U32)
        selu = sb("selu", [2, TOPK], U32)
        selfl = sb("selfl", [2, TOPK])
        e12 = sb("e12", [2, TOPK])
        eidf = sb("eidf", [HEADS, TOPK])
        gsum = sb("gsum", [2, HEADS])
        gn = sb("gn", [HEADS, TOPK])
        gc = sb("gc", [SLOTS])
        idc = sb("idc", [SLOTS], I32)
        zt = sb("zt", [8])
        ge = sb("ge", [8])
        diag = sb("diag", [DIAGS, P])
        warm = sb("warm", [2])

        cand = tmpB[:, 0:256]
        left = tmpB[:, 256:512]
        eqm = tmpB[:, 512:768].rearrange("p (s a) -> p s a", a=TOPK)
        srow = tmpB[:, 768:896]
        qT = tmpA[:].rearrange("p (b q t) -> p b q t", b=2, q=4)
        ws_s = ring[:, 0, 0:GROUPS * P].rearrange("p (g n) -> p g n", g=GROUPS)

        accY = ctx.enter_context(nc.psum_tensor("accY", [P, 2, 512], F32))
        ps = [ctx.enter_context(nc.psum_tensor(f"psF{i}", [P, 512], F32)) for i in range(4)]
        pt = ctx.enter_context(nc.psum_tensor("psT", [P, 2, 512], F32))

        par_in = sem("par_in")
        rows_in = sem("rows_in")
        wq_in = sem("wq_in")
        ws_in = sem("ws_in")
        wsp_in = sem("wsp_in")
        wab_in = sem("wab_in")
        st_in = sem("st_in")
        x_in = sem("x_in")
        w_in_s = [sem("piece_in0"), sem("piece_in1")]
        eps_set = sem("eps_set")
        pool_set = sem("pool_set")
        dve_set = sem("dve_set")
        act_set = sem("act_set")
        dve_step = sem("dve_step")
        act_step = sem("act_step")
        dve_held = sem("dve_held")
        act_held = sem("act_held")
        pool_held = sem("pool_held")
        squares = sem("squares")
        growth_done = sem("growth_done")
        root_done = sem("root_done")
        h_done = sem("h_done")
        turned = sem("turned")
        hT_done = sem("hT_done")
        piece_done = sem("piece_done")
        gelus = sem("gelus")
        v_done = sem("v_done")
        spat_done = sem("spat_done")
        ya_done = sem("ya_done")
        yaT_done = sem("yaT_done")
        xc_done = sem("xc_done")
        gates_done = sem("gates_done")
        exps_done = sem("exps_done")
        rec_done = sem("rec_done")
        decay_done = sem("decay_done")
        yb_done = sem("yb_done")
        ybsq_done = sem("ybsq_done")
        ybT_done = sem("ybT_done")
        ssqb_done = sem("ssqb_done")
        x1_done = sem("x1_done")
        h2_done = sem("h2_done")
        q_done = sem("q_done")
        qT_done = sem("qT_done")
        sc_done = sem("sc_done")
        rows_done = sem("rows_done")
        diff_done = sem("diff_done")
        soft_done = sem("soft_done")
        idx_ready = sem("idx_ready")
        xn_free = sem("xn_free")
        gat = [sem(f"gathered{r}") for r in range(RING)]
        dots = sem("dots")
        egelu = sem("egelu")
        diags = sem("diags")
        vdone = sem("vdone")
        y_taken = sem("y_taken")
        y_sq = sem("y_sq")
        y_ready = sem("y_ready")
        y_out = sem("y_out")
        v_out = sem("v_out")
        st_ready = sem("st_ready")
        st_out = sem("st_out")

        block = ctx.enter_context(nc.Block())

        def col(name, j=0, n=1):
            a = COLS[name][0] + j
            return par[:, a:a + n]

        def many(name, width):
            a, b = COLS[name]
            return par[:, a:b].unsqueeze(2).to_broadcast([P, b - a, width])

        uses = [len(range(r, SLOTS, RING)) for r in range(RING)]

        w_in_v = w_in.rearrange("(c p) n -> p c n", p=P)
        w_out_v = w_out.rearrange("(c p) n -> p c n", p=P)
        pieces = [w_in_v[:, :, 512:1024], w_in_v[:, :, 0:512], w_in_v[:, :, 1024:1536], w_in_v[:, :, 1536:2048],
                  w_out_v[:, :, 0:512], w_out_v[:, :, 512:1024]]

        @block.sync
        def _(sp):
            def load_front(n):
                if n.offset or n.reg is not None:
                    sp.wait_ge(xn_free, n(1, 0))
                sp.dma_start(xn[:], x_all[bass.ds(n(P, 0), P), :]).then_inc(x_in, 16)

            def load_piece(n, k):
                if k >= 2 or n.offset or n.reg is not None:
                    sp.wait_ge(piece_done, n(PIECES, k - 1))
                sp.dma_start(wbuf[:, k % 2], pieces[k]).then_inc(w_in_s[k % 2], 16)

            def store_y(m):
                sp.wait_ge(y_ready, m(1, 1))
                sp.dma_start(y_all[bass.ds(m(P, 0), P), :], x1[:]).then_inc(y_out, 16)

            first = When(0)
            load_front(first)
            sp.dma_start(par[:], cols).then_inc(par_in, 16)
            load_piece(first, 0)
            load_piece(first, 1)
            for k in range(2, PIECES):
                load_piece(first, k)
            sp.dma_start(wq[:], w_q.rearrange("(c p) n -> p c n", p=P)).then_inc(wq_in, 16)
            sp.wait_ge(v_done, 1)
            sp.dma_start(v_rows, vg[:]).then_inc(v_out, 16)
            sp.wait_ge(st_ready, 1)
            sp.dma_start(state_sample, last[:].rearrange("p m s -> p (m s)")).then_inc(st_out, 16)
            with sp.Fori(0, TILES - 1) as i:
                n, m = When(1, i), When(0, i)
                load_front(n)
                for k in range(PIECES):
                    load_piece(n, k)
                store_y(m)
            sp.wait_ge(st_ready, TILES)
            sp.dma_start(state_prompt, last[:].rearrange("p m s -> p (m s)")).then_inc(st_out, 16)
            store_y(When(TILES - 1))
            sp.wait_ge(v_out, 16)
            sp.wait_ge(st_out, 32)
            sp.wait_ge(y_out, 16 * TILES)

        @block.gpsimd
        def _(pool):
            nc.gpsimd.memset(eps[:], EPS).then_inc(eps_set, 1)
            nc.gpsimd.memset(ws_s, 0.0).then_inc(pool_set, 1)
            nc.gpsimd.memset(wab[:], 0.0).then_inc(pool_set, 1)
            nc.gpsimd.memset(wib[:], 0.0).then_inc(pool_set, 1)
            pool.wait_ge(pool_set, 3)
            for b in range(NB):
                pool.dma_start(ws_s[b * NT:(b + 1) * NT, :, b * NT:(b + 1) * NT],
                               ws_t[0:NT, :, 0:NT]).then_inc(ws_in, 16)
            for w, sbw in ((w_a, wab), (w_i, wib)):
                for e in range(2):
                    pool.dma_start(sbw[64 * e:64 * e + 64, :, 64 * e:64 * e + 64],
                                   w.rearrange("(m e) i j -> e i m j", e=2)[e]).then_inc(wab_in, 16)
            pool.dma_start(g_v[:], rows[0:1, 2 * D:2 * D + DH].to_broadcast([P, DH])).then_inc(rows_in, 16)
            pool.dma_start(ws[:], ws_t).then_inc(wsp_in, 16)
            pool.dma_start(xbuf[:].rearrange("p m (b s) -> p m b s", b=NB)[:, :, :, 0:HIST],
                           conv_state).then_inc(st_in, 16)
            pool.dma_start(carry[:], lru_state).then_inc(st_in, 16)
            pool.dma_start(g_ffn[:], rows[0:1, 0:D].to_broadcast([P, D])).then_inc(rows_in, 16)
            pool.dma_start(g_fin[:], rows[0:1, D:2 * D].to_broadcast([P, D])).then_inc(rows_in, 16)
            pool.dma_start(keys[:], keys_t).then_inc(rows_in, 16)
            nc.gpsimd.memset(ones[:], 1.0).then_inc(pool_set, 1)
            nc.gpsimd.iota(iota_i[:], [[1, TOPK]], 0, 0).then_inc(pool_set, 1)
            nc.gpsimd.memset(ident[:], 0.0).then_inc(pool_set, 1)
            pool.wait_ge(pool_set, 6)
            nc.gpsimd.affine_select(out=ident[:], in_=ident[:], compare_op=ALU.not_equal, fill=1.0, base=0,
                                    pattern=[[-1, P]], channel_multiplier=1).then_inc(pool_set, 1)
            pool.wait_ge(ws_in, 16 * NB)
            nc.gpsimd.affine_select(out=ws_s, in_=ws_s, compare_op=ALU.is_ge, fill=0.0, base=0,
                                    pattern=[[0, GROUPS], [1, P]], channel_multiplier=-1).then_inc(pool_set, 1)
            pool.wait_ge(wsp_in, 16)
            nc.gpsimd.affine_select(out=ws[:], in_=ws[:], compare_op=ALU.is_ge, fill=0.0, base=0,
                                    pattern=[[0, GROUPS], [1, P]], channel_multiplier=-1).then_inc(pool_set, 1)

            def gather_tile(m):
                for s in range(SLOTS):
                    if s == 0:
                        pool.wait_ge(idx_ready, m(1, 1))
                        pool.sem_inc(pool_held, 1)
                    before = s - RING if s >= RING else s + (SLOTS - 1 - s) // RING * RING - SLOTS
                    pool.wait_ge(vdone, m(SLOTS, SLOTS + before + 1))
                    pool.sem_inc(pool_held, 1)
                    nc.gpsimd.indirect_dma_start(ring[:, s % RING], None, experts,
                                                 bass.IndirectOffsetOnAxis(ap=idc[:, s:s + 1], axis=0)
                                                 ).then_inc(gat[s % RING], 16)

            with pool.Fori(0, TILES) as i:
                gather_tile(When(0, i))

        @block.vector
        def _(v):
            st = Steps(v, dve_step, dve_held)
            V = nc.vector

            v.sem_inc(diags, SLOTS)
            v.sem_inc(y_taken, 2)
            v.wait_ge(par_in, 16)
            V.tensor_scalar(nbias[:], par[:, COLS["b_a"][0]:COLS["b_i"][1]], -1.0, None, ALU.mult).then_inc(dve_set, 1)
            V.tensor_scalar(lt[:, 0], col("lam", 0, HC), -1.0, None, ALU.mult).then_inc(dve_set, 1)
            v.wait_ge(dve_set, 2)
            V.tensor_tensor(lt[:, 1], lt[:, 0], col("lam", 0, HC), ALU.min).then_inc(dve_set, 1)
            v.wait_ge(act_set, 1)
            V.tensor_scalar(lt[:, 3], lt[:, 2], 2.0, None, ALU.add).then_inc(dve_set, 1)
            v.wait_ge(dve_set, 4)
            V.reciprocal(lt[:, 4], lt[:, 3]).then_inc(dve_set, 1)
            v.wait_ge(dve_set, 5)
            V.tensor_tensor(lt[:, 5], lt[:, 4], lt[:, 2], ALU.mult).then_inc(dve_set, 1)
            v.wait_ge(dve_set, 6)
            V.tensor_tensor(lt[:, 3], lt[:, 5], lt[:, 5], ALU.mult).then_inc(dve_set, 1)
            v.wait_ge(dve_set, 7)
            V.tensor_scalar(lt[:, 4], lt[:, 3], 1.0 / 17.0, None, ALU.mult).then_inc(dve_set, 1)
            done = 8
            for k in (15, 13, 11, 9, 7, 5, 3):
                v.wait_ge(dve_set, done)
                V.scalar_tensor_tensor(out=lt[:, 4], in0=lt[:, 4], scalar=1.0 / k, in1=lt[:, 3], op0=ALU.add,
                                       op1=ALU.mult).then_inc(dve_set, 1)
                done += 1
            v.wait_ge(dve_set, done)
            V.scalar_tensor_tensor(out=lt[:, 4], in0=lt[:, 4], scalar=1.0, in1=lt[:, 5], op0=ALU.add,
                                   op1=ALU.mult).then_inc(dve_set, 1)
            V.tensor_scalar(lt[:, 0], col("lam", 0, HC), 0.0, LRU_C, ALU.min, ALU.mult).then_inc(dve_set, 1)
            done += 2
            v.wait_ge(dve_set, done)
            V.scalar_tensor_tensor(out=lamc[:], in0=lt[:, 4], scalar=-2.0 * LRU_C, in1=lt[:, 0], op0=ALU.mult,
                                   op1=ALU.add).then_inc(dve_set, 1)
            v.wait_ge(pool_set, 7)
            V.tensor_copy(iota[:], iota_i[:]).then_inc(dve_set, 1)
            v.wait_ge(dve_set, done + 2)

            def rstd(n, j):
                st.step(V.reciprocal(rs[:, j:j + 1], rms[:, j:j + 1]), n)

            def front(p, n, sample):
                xs = xbuf[:].rearrange("p m (b s) -> p m b s", b=NB)

                def tap(m, k):
                    return xs[:, m, :, k:k + NT] if sample else xbuf[:, m, k:k + P]

                def seg(t):
                    return t.rearrange("p m (b s) -> p m b s", b=NB if sample else 1)

                if p == 1:
                    v.wait_ge(squares, n(NORMS, 2))
                    rstd(n, 0)
                    st.after()
                    st.gives(V.tensor_scalar(tmpA[:], xn[:], rs[:, 0:1], None, ALU.mult), h_done, n(1, 1))
                if p in (3, 35):
                    second = p == 35
                    v.wait_ge(turned, n(3, 3 if second else 1))
                    for b in range(2):
                        out = hT[:, 4 * b:4 * b + 4, :]
                        src = pt[:, b].rearrange("p (c t) -> p c t", c=4)
                        if second:
                            ins = V.tensor_copy(out, src)
                        else:
                            g = par[:, 4 * b:4 * b + 4].unsqueeze(2).to_broadcast([P, 4, P])
                            ins = V.tensor_tensor(out, src, g, ALU.mult)
                        if b == 0:
                            st.step(ins, n)
                        else:
                            st.gives(ins, hT_done, n(2, 2 if second else 1))
                if p == 6:
                    v.wait_ge(squares, n(NORMS, 4))
                    rstd(n, 1)
                    if sample:
                        v.wait_ge(rows_in, 64)
                    st.after()
                    st.gives(V.scalar_tensor_tensor(out=vg[:], in0=vg[:], scalar=rs[:, 1:2], in1=g_v[:], op0=ALU.mult,
                                                    op1=ALU.mult), v_done, n(1, 1))
                if p == 10:
                    v.wait_ge(spat_done, n(1, 1))
                    v.wait_ge(gelus, n(3, 2))
                    for g in range(GROUPS):
                        a = slice(g * P, g * P + P)
                        ins = V.scalar_tensor_tensor(out=ug[:, a], in0=ps[0][:, a],
                                                     scalar=col("bs_sample" if sample else "bs_prompt", g),
                                                     in1=ug[:, a], op0=ALU.add, op1=ALU.mult)
                        if g < GROUPS - 1:
                            st.step(ins, n)
                        else:
                            st.gives(ins, ya_done, n(1, 1))
                if p == 12:
                    v.wait_ge(turned, n(3, 2))
                    if sample:
                        v.wait_ge(v_out, 16)
                    st.gives(V.tensor_tensor(vg[:].rearrange("p (m t) -> p m t", m=HC),
                                             pt[:, 0].rearrange("p (c t) -> p c t", c=4), many("g_a", P), ALU.mult),
                             yaT_done, n(1, 1))
                if p == 13:
                    v.wait_ge(piece_done, n(PIECES, 3))
                    if sample:
                        v.wait_ge(st_in, 32)
                    for m in range(HC):
                        src = ps[2][:, m * P:(m + 1) * P]
                        out = xs[:, m, :, HIST:SEGS] if sample else xbuf[:, m, HIST:HIST + P]
                        if sample:
                            src = src.rearrange("p (b s) -> p b s", b=NB)
                        st.step(V.tensor_copy(out, src), n)
                if p in (13, 14):
                    for m in (0, 1) if p == 13 else (2, 3):
                        out = seg(xc[:])[:, m] if sample else xc[:, m]
                        st.after()
                        st.step(V.tensor_scalar(out, tap(m, 0), col("conv_w", m * TAPS), col("conv_b", m), ALU.mult,
                                                ALU.add), n)
                        for k in range(1, TAPS):
                            st.after()
                            ins = V.scalar_tensor_tensor(out=out, in0=tap(m, k), scalar=col("conv_w", m * TAPS + k),
                                                         in1=out, op0=ALU.mult, op1=ALU.add)
                            if (m, k) == (HC - 1, TAPS - 1):
                                st.gives(ins, xc_done, n(1, 1))
                            else:
                                st.step(ins, n)
                if p == 15:
                    st.after()
                    if sample:
                        st.step(V.tensor_copy(last[:, :, 0:NB * HIST].rearrange("p m (b k) -> p m b k", b=NB),
                                              xs[:, :, :, NT:SEGS]), n)
                        st.after()
                        st.step(V.memset(xbuf[:, :, 0:HIST], 0.0), n)
                    else:
                        st.step(V.tensor_copy(last[:, :, 0:HIST], xbuf[:, :, P:P + HIST]), n)
                        st.after()
                        st.step(V.tensor_copy(xbuf[:, :, 0:HIST], last[:, :, 0:HIST]), n)
                if p == 17:
                    v.wait_ge(exps_done, n(1, 1))
                    st.step(V.tensor_scalar(tmpA[:], tmpA[:], 1.0, None, ALU.add), n)
                    st.after()
                    st.gives(V.reciprocal(tmpA[:], tmpA[:]), rec_done, n(1, 1))
                th, a_t = tmpB[:, 0:DH], tmpB[:, DH:D]
                r_t, i_t = tmpA[:, 0:DH], tmpA[:, DH:D]
                if p == 18:
                    st.after()
                    st.step(V.tensor_tensor(i_t, i_t, xc[:].rearrange("p m t -> p (m t)"), ALU.mult), n)
                if p == 19:
                    v.wait_ge(decay_done, n(1, 1))
                    st.step(V.tensor_scalar(r_t, th, -1.0, 1.0, ALU.mult, ALU.add), n)
                    st.after()
                    st.step(V.reciprocal(r_t, r_t), n)
                    st.after()
                    st.gives(V.tensor_tensor(th, th, r_t, ALU.mult), growth_done, n(1, 1))
                if p == 21:
                    v.wait_ge(root_done, n(1, 1))
                    st.step(V.tensor_tensor(i_t, i_t, th, ALU.mult), n)
                if p == 21:
                    nb = NB if sample else 1
                    a4 = seg(a_t.rearrange("p (m t) -> p m t", m=HC))[:, :, :, 0]
                    b4 = seg(i_t.rearrange("p (m t) -> p m t", m=HC))[:, :, :, 0]
                    st.after()
                    st.step(V.tensor_tensor(cin[:, :, 0:nb], a4, carry[:, :, 0:nb], ALU.mult), n)
                    st.after()
                    st.step(V.tensor_tensor(b4, b4, cin[:, :, 0:nb], ALU.add), n)
                    st.after()
                    st.step(V.tensor_scalar(a4, a4, 0.0, None, ALU.mult), n)
                    for m in range(HC):
                        c = slice(m * P, m * P + P)
                        st.after()
                        st.step(V.tensor_tensor_scan(hl[:, m], a_t[:, c], i_t[:, c], 0.0, ALU.mult, ALU.add), n)
                if p == 22:
                    st.after()
                    if sample:
                        st.step(V.tensor_copy(last[:, :, NB * HIST:], seg(hl)[:, :, :, NT - 1]), n)
                        st.after()
                        st.gives(V.memset(carry[:, :, 0:1], 0.0), st_ready, n(1, 1))
                    else:
                        st.step(V.tensor_copy(carry[:, :, 0:1], hl[:, :, P - 1:P]), n)
                        st.after()
                        st.gives(V.tensor_copy(last[:, :, HIST:HIST + 1], carry[:, :, 0:1]), st_ready, n(1, 1))
                    st.after()
                    v.wait_ge(gelus, n(3, 3))
                    st.gives(V.tensor_tensor(hl, hl, gg[:], ALU.mult), yb_done, n(1, 1))
                if p == 23:
                    st.after()
                    st.gives(V.tensor_tensor(xc[:], hl, many("g_b", P), ALU.mult), ybT_done, n(1, 1))
                if p == 25:
                    v.wait_ge(squares, n(NORMS, 7))
                    rstd(n, 2)
                    rstd(n, 3)
                if p in (28, 31):
                    j = 0 if p == 28 else 1
                    v.wait_ge(piece_done, n(PIECES, 5 + j))
                    c = slice(j * 512, j * 512 + 512)
                    st.after()
                    st.step(V.scalar_tensor_tensor(out=xn[:, c], in0=ps[2 * j][:], scalar=rs[:, 2:3], in1=xn[:, c],
                                                   op0=ALU.mult, op1=ALU.add), n)
                    st.after()
                    ins = V.scalar_tensor_tensor(out=xn[:, c], in0=ps[2 * j + 1][:], scalar=rs[:, 3:4], in1=xn[:, c],
                                                 op0=ALU.mult, op1=ALU.add)
                    if j:
                        st.gives(ins, x1_done, n(1, 1))
                    else:
                        st.step(ins, n)
                if p == 33:
                    v.wait_ge(squares, n(NORMS, 9))
                    rstd(n, 4)
                    st.after()
                    st.gives(V.scalar_tensor_tensor(out=h2n[:], in0=xn[:], scalar=rs[:, 4:5], in1=g_ffn[:],
                                                    op0=ALU.mult, op1=ALU.mult), h2_done, n(1, 1))
                for r in range(4):
                    row = p - (40 + 5 * r)
                    if 0 <= row < 4:
                        half = row % 2
                        sc = ps[r][:, row * P:(row + 1) * P]
                        if row == 0:
                            v.wait_ge(sc_done, n(4, r + 1))
                        for t in range(2):
                            src = sc if t == 0 else srow
                            o = slice(8 * t, 8 * t + 8)
                            st.after_held()
                            st.step(V.max(vals[:, half, o], src), n)
                            st.after_held()
                            if t == 1 and row == 3:
                                st.gives(V.max_index(idx8[:, half, o], vals[:, half, o], src), rows_done, n(4, r + 1))
                            else:
                                st.step(V.max_index(idx8[:, half, o], vals[:, half, o], src), n)
                            if t == 0:
                                st.after_held()
                                st.step(V.match_replace(srow, vals[:, half, o], sc, LOWEST), n)
                        if half == 1:
                            choose(2 * r + row // 2, n)
                if p == 61:
                    st.after()
                    st.gives(V.tensor_tensor(gn[:], best[:], best[:, :, 0:1].to_broadcast([P, HEADS, TOPK]),
                                             ALU.subtract), diff_done, n(1, 1))
                if p == 62:
                    v.wait_ge(soft_done, n(1, 1))
                    st.step(V.tensor_reduce(gsum[:, 0], gn[:], AX_X, ALU.add), n)
                    st.after()
                    st.step(V.reciprocal(gsum[:, 1], gsum[:, 0]), n)
                    st.after()
                    st.step(V.tensor_tensor(gn[:], gn[:], gsum[:, 1].unsqueeze(2).to_broadcast([P, HEADS, TOPK]),
                                            ALU.mult), n)

            def choose(h, n):
                st.after()
                st.step(V.tensor_copy(idxf[:], idx8[:]), n)
                st.step(V.tensor_tensor(cand.rearrange("p (a b) -> p a b", a=TOPK),
                                        vals[:, 0].unsqueeze(2).to_broadcast([P, TOPK, TOPK]),
                                        vals[:, 1].unsqueeze(1).to_broadcast([P, TOPK, TOPK]), ALU.add), n)
                for t in range(2):
                    src = cand if t == 0 else left
                    o = slice(8 * t, 8 * t + 8)
                    st.after_held()
                    st.step(V.max(best[:, h, o], src), n)
                    st.after_held()
                    st.step(V.max_index(sel[:, o], best[:, h, o], src), n)
                    if t == 0:
                        st.after_held()
                        st.step(V.match_replace(left, best[:, h, o], cand, LOWEST), n)
                st.after()
                st.step(V.tensor_scalar(selu[:, 0], sel[:], 4, None, ALU.logical_shift_right), n)
                st.step(V.tensor_scalar(selu[:, 1], sel[:], TOPK - 1, None, ALU.bitwise_and), n)
                st.after()
                st.step(V.tensor_copy(selfl[:], selu[:]), n)
                for half in range(2):
                    st.after()
                    st.step(V.tensor_tensor(eqm, selfl[:, half].unsqueeze(2).to_broadcast([P, TOPK, TOPK]),
                                            iota[:].unsqueeze(1).to_broadcast([P, TOPK, TOPK]), ALU.is_equal), n)
                    st.after()
                    st.step(V.tensor_tensor(eqm, eqm, idxf[:, half].unsqueeze(1).to_broadcast([P, TOPK, TOPK]),
                                            ALU.mult), n)
                    st.after()
                    st.step(V.tensor_reduce(e12[:, half], eqm, AX_X, ALU.add), n)
                st.after()
                st.step(V.scalar_tensor_tensor(out=eidf[:, h], in0=e12[:, 0], scalar=float(P), in1=e12[:, 1],
                                               op0=ALU.mult, op1=ALU.add), n)

            def dot_pair(g, m):
                for s in (2 * g, 2 * g + 1):
                    v.wait_ge(gat[s % RING], m(16 * uses[s % RING], 16 * (s // RING + 1)))
                    if s % 2 == 0:
                        v.wait_ge(egelu, m(PAIRS, PAIRS + g - 3))
                    V.tensor_tensor_reduce(out=ring[:, s % RING, 0:D], in0=ring[:, s % RING, 0:D], in1=h2[:],
                                           scale=1.0, scalar=0.0, op0=ALU.mult, op1=ALU.add,
                                           accum_out=zt[:, s % 8:s % 8 + 1]).then_inc(dots, 1)

            def diag_pair(g, m):
                v.wait_ge(egelu, m(PAIRS, PAIRS + g + 1))
                for s in (2 * g, 2 * g + 1):
                    v.wait_ge(vdone, m(SLOTS, SLOTS + s - DIAGS + 1))
                    V.tensor_scalar(diag[:, s % DIAGS], ident[:], ge[:, s % 8:s % 8 + 1], gc[:, s:s + 1], ALU.mult,
                                    ALU.mult).then_inc(diags, 1)

            def adopt_indices(m):
                st.after()
                st.gives(V.tensor_copy(idc[:], eidf[:].rearrange("p h k -> p (h k)")), idx_ready, m(1, 1))

            def adopt_rest(m):
                st.after()
                st.step(V.tensor_copy(gc[:], gn[:].rearrange("p h k -> p (h k)")), m)
                st.step(V.tensor_copy(h2[:], h2n[:]), m)

            def adopt_x(m):
                st.after()
                st.gives(V.tensor_copy(x1[:], xn[:]), xn_free, m(1, 1))

            def finish(m):
                v.wait_ge(vdone, m(SLOTS, 2 * SLOTS))
                V.tensor_tensor(x1[:], x1[:], accY[:].rearrange("p a b -> p (a b)"), ALU.add).then_inc(y_taken, 1)
                v.wait_ge(y_sq, m(2, 2))
                V.reciprocal(yrms[:, 2:3], yrms[:, 1:2]).then_inc(y_taken, 1)
                v.wait_ge(y_taken, m(2, 4))
                V.scalar_tensor_tensor(out=x1[:], in0=x1[:], scalar=yrms[:, 2:3], in1=g_fin[:], op0=ALU.mult,
                                       op1=ALU.mult).then_inc(y_ready, 1)

            first = When(0)
            for p in range(PAIRS):
                front(p, first, True)
            st.per = st.count + 0
            adopt_indices(first)
            adopt_rest(first)
            adopt_x(first)
            per = st.count
            st.per = per
            with v.Fori(0, TILES - 1) as i:
                n, m = When(1, i), When(0, i)
                st.count = 0
                for g in range(PAIRS):
                    dot_pair(g, m)
                    if g == 0:
                        st.last = (xn_free, n(1, 0))
                    if g >= 1:
                        diag_pair(g - 1, m)
                    front(g, n, False)
                adopt_indices(n)
                diag_pair(PAIRS - 1, m)
                v.wait_ge(diags, m(SLOTS, 2 * SLOTS))
                adopt_rest(n)
                finish(m)
                v.wait_ge(y_out, m(16, 16))
                adopt_x(n)
                assert st.count == per, (st.count, per)
            m = When(TILES - 1)
            for g in range(PAIRS):
                dot_pair(g, m)
                if g >= 1:
                    diag_pair(g - 1, m)
            diag_pair(PAIRS - 1, m)
            finish(m)

        @block.scalar
        def _(a):
            st = Steps(a, act_step, act_held)
            A = nc.scalar

            a.sem_inc(egelu, PAIRS)
            a.wait_ge(eps_set, 1)
            a.wait_ge(dve_set, 3)
            A.activation(lt[:, 2], lt[:, 1], ACT.Exp).then_inc(act_set, 1)

            def mean_root(n, k, junk, src, j, width):
                A.activation(junk, src, ACT.Square, accum_out=ssq[:, j:j + 1]).then_inc(squares, 1)
                a.wait_ge(squares, n(NORMS, k))
                A.activation(rms[:, j:j + 1], ssq[:, j:j + 1], ACT.Sqrt, bias=eps[:, 0:1],
                             scale=1.0 / width).then_inc(squares, 1)

            def front(p, n):
                if p == 0:
                    a.wait_ge(x_in, n(16, 16))
                    mean_root(n, 1, tmpA[:], xn[:], 0, D)
                if p == 5:
                    a.wait_ge(piece_done, n(PIECES, 1))
                    A.activation(vg[:], ps[0][:], ACT.Gelu_apprx_tanh).then_inc(gelus, 1)
                    a.wait_ge(gelus, n(3, 1))
                    mean_root(n, 3, tmpB[:, 0:DH], vg[:], 1, DH)
                if p == 8:
                    a.wait_ge(piece_done, n(PIECES, 2))
                    A.activation(ug[:], ps[1][:], ACT.Gelu_apprx_tanh).then_inc(gelus, 1)
                if p == 11:
                    a.wait_ge(ya_done, n(1, 1))
                    mean_root(n, 5, tmpB[:, DH:D], ug[:], 2, DH)
                if p == 14:
                    a.wait_ge(piece_done, n(PIECES, 4))
                    A.activation(gg[:].rearrange("p m t -> p (m t)"), ps[3][:], ACT.Gelu_apprx_tanh).then_inc(gelus, 1)
                if p == 16:
                    a.wait_ge(gates_done, n(1, 1))
                    for j in range(2 * HC):
                        ins = A.activation(tmpA[:, j * P:(j + 1) * P], pt[:, j // HC, (j % HC) * P:(j % HC + 1) * P],
                                           ACT.Exp, bias=nbias[:, j:j + 1], scale=-1.0)
                    ins.then_inc(exps_done, 1)
                if p == 18:
                    a.wait_ge(rec_done, n(1, 1))
                    for f, o in ((ACT.Tanh, 0), (ACT.Exp, DH)):
                        for m in range(HC):
                            ins = A.activation(tmpB[:, o + m * P:o + (m + 1) * P], tmpA[:, m * P:(m + 1) * P], f,
                                               scale=lamc[:, m:m + 1])
                    ins.then_inc(decay_done, 1)
                if p == 23:
                    a.wait_ge(yb_done, n(1, 1))
                    A.activation(tmpA[:, 0:DH], hl.rearrange("p m t -> p (m t)"), ACT.Square).then_inc(ybsq_done, 1)
                if p == 20:
                    a.wait_ge(growth_done, n(1, 1))
                    A.activation(tmpB[:, 0:DH], tmpB[:, 0:DH], ACT.Sqrt, scale=-2.0).then_inc(root_done, 1)
                if p == 24:
                    a.wait_ge(ssqb_done, n(1, 1))
                    A.activation(rms[:, 3:4], pt[:, 1, 0:1], ACT.Sqrt, bias=eps[:, 0:1], scale=1.0 / DH
                                 ).then_inc(squares, 1)
                if p == 32:
                    a.wait_ge(x1_done, n(1, 1))
                    mean_root(n, 8, tmpB[:], xn[:], 4, D)
                for r in range(4):
                    if p == 38 + 5 * r:
                        a.wait_ge(q_done, n(4, r + 1))
                        if r >= 2:
                            a.wait_ge(sc_done, n(4, r - 1))
                        A.activation(qT[:, r % 2].rearrange("p q t -> p (q t)"), pt[:, r % 2], ACT.Copy
                                     ).then_inc(qT_done, 1)
                if p == 62:
                    a.wait_ge(diff_done, n(1, 1))
                    A.activation(gn[:], gn[:], ACT.Exp).then_inc(soft_done, 1)

            def gelu_pair(g, m):
                a.wait_ge(dots, m(SLOTS, 2 * g + 2))
                o = 2 * g % 8
                a.wait_ge(diags, m(SLOTS, SLOTS + 2 * g - 6))
                A.activation(ge[:, o:o + 2], zt[:, o:o + 2], ACT.Gelu_apprx_tanh).then_inc(egelu, 1)

            def square_y(m):
                a.wait_ge(y_taken, m(2, 3))
                A.activation(tmpB[:], x1[:], ACT.Square, accum_out=yrms[:, 0:1]).then_inc(y_sq, 1)
                a.wait_ge(y_sq, m(2, 1))
                A.activation(yrms[:, 1:2], yrms[:, 0:1], ACT.Sqrt, bias=eps[:, 0:1], scale=1.0 / D
                             ).then_inc(y_sq, 1)

            for p in range(PAIRS):
                front(p, When(0))
            with a.Fori(0, TILES - 1) as i:
                n, m = When(1, i), When(0, i)
                for g in range(PAIRS):
                    gelu_pair(g, m)
                    front(g, n)
                square_y(m)
            m = When(TILES - 1)
            for g in range(PAIRS):
                gelu_pair(g, m)
            square_y(m)

        @block.tensor
        def _(t):
            T = nc.tensor

            def piece(n, k):
                if k == 0:
                    t.wait_ge(hT_done, n(2, 1))
                if k == 4:
                    t.wait_ge(squares, n(NORMS, 7))
                    t.wait_ge(yaT_done, n(1, 1))
                t.wait_ge(w_in_s[k % 2], n(3 * 16, 16 * (k // 2 + 1)))
                w = wbuf[:, k % 2]
                if k < 2:
                    for c in range(DC):
                        ins = T.matmul(ps[k][:], hT[:, c], w[:, c], start=c == 0, stop=c == DC - 1)
                elif k < 4:
                    for m in range(HC):
                        for c in range(DC):
                            ins = T.matmul(ps[k][:, m * P:(m + 1) * P], w[:, c, m * P:(m + 1) * P], hT[:, c],
                                           start=c == 0, stop=c == DC - 1)
                else:
                    j = k - 4
                    for c in range(HC):
                        T.matmul(ps[2 * j][:], vg[:, c * P:(c + 1) * P], w[:, c], start=c == 0, stop=c == HC - 1)
                    for c in range(HC):
                        ins = T.matmul(ps[2 * j + 1][:], xc[:, c], w[:, HC + c], start=c == 0, stop=c == HC - 1)
                ins.then_inc(piece_done, 1)

            def front(p, n, sample):
                if p in (2, 34):
                    src = tmpA if p == 2 else h2n
                    if p == 2:
                        t.wait_ge(h_done, n(1, 1))
                    else:
                        t.wait_ge(h2_done, n(1, 1))
                    if p == 2 and sample:
                        t.wait_ge(pool_set, 7)
                    for c in range(DC):
                        ins = T.transpose(pt[:, c // 4, (c % 4) * P:(c % 4 + 1) * P], src[:, c * P:(c + 1) * P],
                                          ident[:])
                    ins.then_inc(turned, 1)
                for pos, k in ((4, 0), (7, 1), (10, 2), (13, 3), (26, 4), (29, 5)):
                    if p == pos:
                        piece(n, k)
                if p == 9:
                    t.wait_ge(v_done, n(1, 1))
                    if sample:
                        t.wait_ge(pool_set, 9)
                    for g in range(GROUPS):
                        ins = T.matmul(ps[0][:, g * P:(g + 1) * P], (ws_s if sample else ws)[:, g],
                                       vg[:, g * P:(g + 1) * P], start=True, stop=True)
                    ins.then_inc(spat_done, 1)
                if p == 11:
                    t.wait_ge(ya_done, n(1, 1))
                    for c in range(HC):
                        ins = T.transpose(pt[:, 0, c * P:(c + 1) * P], ug[:, c * P:(c + 1) * P], ident[:])
                    ins.then_inc(turned, 1)
                if p == 15:
                    t.wait_ge(xc_done, n(1, 1))
                    if sample:
                        t.wait_ge(wab_in, 64)
                    for j, w in enumerate((wab, wib)):
                        for m in range(HC):
                            ins = T.matmul(pt[:, j, m * P:(m + 1) * P], w[:, m], xc[:, m], start=True, stop=True)
                    ins.then_inc(gates_done, 1)
                if p == 24:
                    t.wait_ge(ybsq_done, n(1, 1))
                    for c in range(HC):
                        ins = T.matmul(pt[:, 1, 0:1], tmpA[:, c * P:(c + 1) * P], ones[:, 0:1], start=c == 0,
                                       stop=c == HC - 1)
                    ins.then_inc(ssqb_done, 1)
                    t.wait_ge(ybT_done, n(1, 1))
                for r in range(4):
                    if p == 36 + 5 * r:
                        if r == 0:
                            t.wait_ge(hT_done, n(2, 2))
                            if sample:
                                t.wait_ge(wq_in, 16)
                        if r >= 2:
                            t.wait_ge(qT_done, n(4, r - 1))
                        for q in range(4):
                            for c in range(DC):
                                ins = T.matmul(pt[:, r % 2, q * P:(q + 1) * P],
                                               wq[:, c, (4 * r + q) * P:(4 * r + q + 1) * P], hT[:, c],
                                               start=c == 0, stop=c == DC - 1)
                        ins.then_inc(q_done, 1)
                    if p == 39 + 5 * r:
                        t.wait_ge(qT_done, n(4, r + 1))
                        if sample and r == 0:
                            t.wait_ge(rows_in, 64)
                        for q in range(4):
                            ins = T.matmul(ps[r][:, q * P:(q + 1) * P], qT[:, r % 2, q], keys[:, q % 2], start=True,
                                           stop=True)
                        ins.then_inc(sc_done, 1)

            def weigh_pair(g, m):
                if g == 0:
                    t.wait_ge(y_taken, m(2, 1))
                for s in (2 * g, 2 * g + 1):
                    t.wait_ge(diags, m(SLOTS, SLOTS + s + 1))
                    for j in range(2):
                        ins = T.matmul(accY[:, j], diag[:, s % DIAGS], ring[:, s % RING, D + j * 512:D + (j + 1) * 512],
                                       start=s == 0, stop=s == SLOTS - 1)
                    ins.then_inc(vdone, 1)

            t.sem_inc(vdone, SLOTS)
            for p in range(PAIRS):
                front(p, When(0), True)
            with t.Fori(0, TILES - 1) as i:
                n, m = When(1, i), When(0, i)
                for g in range(PAIRS):
                    weigh_pair(g, m)
                    front(g, n, False)
            m = When(TILES - 1)
            for g in range(PAIRS):
                weigh_pair(g, m)


def kernel(**inputs):
    import numpy as np
    import concourse.bacc as bacc
    from concourse.bass_utils import run_bass_kernel_spmd

    a = {k: np.asarray(x) for k, x in inputs.items()}

    def by_channel(x):
        x = x.reshape(x.shape[:-1] + (x.shape[-1] // P, P))
        return np.moveaxis(x, (-1, -2), (0, 1)).reshape(P, -1)

    bs = a["b_s"][0].T
    cols = np.concatenate([
        by_channel(a["g_mix"][0]), by_channel(a["g_out_a"][0]), by_channel(a["g_out_b"][0]),
        by_channel(a["conv_w"][0]), by_channel(a["conv_b"][0]), by_channel(a["b_a"][0]), by_channel(a["b_i"][0]),
        by_channel(a["lam"][0]), bs, np.concatenate([bs[0:NT]] * NB, axis=0)], axis=1)
    feed = {
        "x_all": np.concatenate([a["x_sample"].reshape(NB * NT, D), a["x_prompt"].reshape(-1, D)], axis=0),
        "cols": cols,
        "conv_state": by_channel(a["state_conv"][0]).reshape(P, HC, NB, HIST),
        "lru_state": by_channel(a["state_lru"][0]).reshape(P, HC, NB),
        "w_in": a["w_in"][0], "w_out": a["w_out"][0], "w_q": a["w_q"][0],
        "ws_t": np.transpose(a["w_s"][0], (2, 0, 1)),
        "w_a": a["w_a"][0], "w_i": a["w_i"][0],
        "keys_t": np.stack([a["k_sub1"][0].T, a["k_sub2"][0].T], axis=1),
        "rows": np.concatenate([a["g_ffn"][0], a["g_final"], a["g_v"][0]])[None, :],
        "experts": np.concatenate([a["u_tab"][0], a["v_tab"][0]], axis=1),
    }
    feed = {k: np.ascontiguousarray(x) for k, x in feed.items()}
    nc = bacc.Bacc("TRN2", target_bir_lowering=False, num_devices=1)
    args = [nc.dram_tensor(k, x.shape, mybir.dt.from_np(x.dtype), kind="ExternalInput").ap() for k, x in feed.items()]
    outs = {"y_all": (TILES * P, D), "v_rows": (P, DH), "state_sample": (P, HC * NB * (HIST + 1)),
            "state_prompt": (P, HC * NB * (HIST + 1))}
    args += [nc.dram_tensor(k, s, F32, kind="ExternalOutput").ap() for k, s in outs.items()]
    hybrid_layer(nc, *args)
    got = run_bass_kernel_spmd(nc, [feed], core_ids=[0]).results[0]
    y = got["y_all"]
    ss = got["state_sample"].reshape(P, HC, NB * (HIST + 1))
    sp = got["state_prompt"].reshape(P, HC, NB * (HIST + 1))

    def channels(x):
        x = np.moveaxis(x, (1, 0), (-2, -1))
        return np.ascontiguousarray(x.reshape(x.shape[:-2] + (DH,)))

    conv_s = channels(ss[:, :, 0:NB * HIST].reshape(P, HC, NB, HIST))[None]
    lru_s = channels(ss[:, :, NB * HIST:])[None]
    conv_p = channels(sp[:, :, 0:HIST])[None, None]
    lru_p = channels(sp[:, :, HIST])[None, None]
    return (y[P:].reshape(1, -1, D), y[0:P].reshape(NB, NT, D), conv_p, lru_p, conv_s, lru_s,
            got["v_rows"].reshape(1, NB, NT, DH))
```

```python
from contextlib import ExitStack

import concourse.bass as bass
from concourse import mybir

F32 = mybir.dt.float32
I32 = mybir.dt.int32
U32 = mybir.dt.uint32
ALU = mybir.AluOpType
ACT = mybir.ActivationFunctionType
AX_X = mybir.AxisListType.X

P = 128
D = 1024
DC = D // P
DH = 512
HC = DH // P
GROUPS = 4
TILES = 5
NB, NT = 8, 16
TAPS = 4
HIST = TAPS - 1
SEGS = NT + HIST
HEADS = 8
TOPK = 16
SLOTS = HEADS * TOPK
RING = 8
PAIRS = SLOTS // 2
LEAD = 4
STEPS = PAIRS - LEAD
EARLY = {45: 0, 47: 1, 49: 2, 51: 3}
CHOOSE_AT = [41 + 5 * (h // 2) + 2 * (h % 2) for h in range(HEADS - 1)] + [PAIRS - LEAD - 1]
DIAGS = 4
PW = 256
PIECES = 12
NORMS = 9
EPS = 1e-6
LOWEST = -3.0e38
LRU_C = 8.0

COLS = {}
_at = 0
for _name, _n in (("g_mix", DC), ("g_a", HC), ("g_b", HC), ("conv_w", HC * TAPS), ("conv_b", HC), ("b_a", HC),
                  ("b_i", HC), ("lam", HC), ("bs_prompt", GROUPS), ("bs_sample", GROUPS)):
    COLS[_name] = (_at, _at + _n)
    _at += _n
NCOLS = _at


class When:

    def __init__(self, offset, reg=None):
        self.offset, self.reg = offset, reg

    def __call__(self, per, k):
        fixed = self.offset * per + k
        return fixed if self.reg is None else self.reg * per + fixed


class Steps:

    def __init__(self, eng, own, held):
        self.eng, self.own, self.held = eng, own, held
        self.per, self.count, self.last = 0, 0, None

    def after(self):
        if self.last is not None:
            self.eng.wait_ge(*self.last)

    def after_held(self):
        self.after()
        self.eng.sem_inc(self.held, 1)

    def step(self, ins, n):
        self.count += 1
        ins.then_inc(self.own, 1)
        self.last = (self.own, n(self.per, self.count))

    def gives(self, ins, sem, value):
        ins.then_inc(sem, 1)
        self.last = (sem, value)


def hybrid_layer(nc, x_all, cols, conv_state, lru_state, w_in, w_out, w_q, ws_t, w_a, w_i, keys_t, rows, experts,
                 y_all, v_rows, state_sample, state_prompt):
    with ExitStack() as ctx:
        def sb(name, shape, dt=F32):
            return ctx.enter_context(nc.sbuf_tensor(name, [P] + shape, dt))

        def sem(name):
            return ctx.enter_context(nc.semaphore(name))

        ring = sb("ring", [RING, 2 * D])
        wbuf = sb("wbuf", [2, DC, PW])
        wq = sb("wq", [DC, 2 * SLOTS * TOPK // 2])
        xn = sb("xn", [D])
        h2n = sb("h2n", [D])
        x1 = sb("x1", [D])
        h2 = sb("h2", [D])
        hT = sb("hT", [DC, P])
        tmpA = sb("tmpA", [D])
        tmpB = sb("tmpB", [D])
        ug = sb("ug", [DH])
        vg = sb("vg", [DH])
        gg = sb("gg", [HC, P])
        xbuf = sb("xbuf", [HC, NB * SEGS])
        xc = sb("xc", [HC, P])
        hl = ug[:].rearrange("p (m t) -> p m t", m=HC)
        g_ffn = sb("g_ffn", [D])
        g_fin = sb("g_fin", [D])
        g_v = sb("g_v", [DH])
        ws = sb("ws", [GROUPS, P])
        wab = sb("wab", [HC, P])
        wib = sb("wib", [HC, P])
        keys = sb("keys", [2, P])
        ident = sb("ident", [P])
        ones = sb("ones", [2])
        iota_i = sb("iota_i", [TOPK], I32)
        iota = sb("iota", [TOPK])
        par = sb("par", [NCOLS])
        nbias = sb("nbias", [2 * HC])
        lamc = sb("lamc", [HC])
        lt = sb("lt", [6, HC])
        carry = sb("carry", [HC, NB])
        cin = sb("cin", [HC, NB])
        last = sb("last", [HC, NB * (HIST + 1)])
        ssq = sb("ssq", [8])
        rms = sb("rms", [8])
        rs = sb("rs", [8])
        eps = sb("eps", [1])
        yrms = sb("yrms", [4])
        vals = sb("vals", [2, TOPK])
        idx8 = sb("idx8", [2, TOPK], U32)
        idxf = sb("idxf", [2, TOPK])
        best = sb("best", [2, TOPK])
        nmax = sb("nmax", [2])
        gexp = sb("gexp", [2, TOPK])
        sel = sb("sel", [TOPK], U32)
        selu = sb("selu", [2, TOPK], U32)
        selfl = sb("selfl", [2, TOPK])
        e12 = sb("e12", [2, TOPK])
        gsum = sb("gsum", [4])
        gc = sb("gc", [SLOTS])
        idc = sb("idc", [SLOTS], I32)
        zt = sb("zt", [8])
        ge = sb("ge", [8])
        diag = sb("diag", [DIAGS, P])
        warm = sb("warm", [2])

        cand = tmpB[:, 0:256]
        left = tmpB[:, 256:512]
        eqm = tmpB[:, 512:768].rearrange("p (s a) -> p s a", a=TOPK)
        srow = tmpB[:, 768:896]
        qT = tmpA[:].rearrange("p (b q t) -> p b q t", b=2, q=4)
        ws_s = ring[:, 0, 0:GROUPS * P].rearrange("p (g n) -> p g n", g=GROUPS)

        accY = ctx.enter_context(nc.psum_tensor("accY", [P, 2, 512], F32))
        ps = [ctx.enter_context(nc.psum_tensor(f"psF{i}", [P, 512], F32)) for i in range(4)]
        pt = ctx.enter_context(nc.psum_tensor("psT", [P, 2, 512], F32))

        par_in = sem("par_in")
        rows_in = sem("rows_in")
        wq_in = sem("wq_in")
        ws_in = sem("ws_in")
        wsp_in = sem("wsp_in")
        wab_in = sem("wab_in")
        st_in = sem("st_in")
        x_in = sem("x_in")
        w_in_s = [sem("piece_in0"), sem("piece_in1")]
        eps_set = sem("eps_set")
        pool_set = sem("pool_set")
        dve_set = sem("dve_set")
        act_set = sem("act_set")
        dve_step = sem("dve_step")
        act_step = sem("act_step")
        dve_held = sem("dve_held")
        act_held = sem("act_held")
        pool_held = sem("pool_held")
        squares = sem("squares")
        growth_done = sem("growth_done")
        root_done = sem("root_done")
        h_done = sem("h_done")
        turned = sem("turned")
        hT_done = sem("hT_done")
        piece_done = sem("piece_done")
        gelus = sem("gelus")
        v_done = sem("v_done")
        spat_done = sem("spat_done")
        ya_done = sem("ya_done")
        yaT_done = sem("yaT_done")
        xc_done = sem("xc_done")
        gates_done = sem("gates_done")
        exps_done = sem("exps_done")
        rec_done = sem("rec_done")
        decay_done = sem("decay_done")
        yb_done = sem("yb_done")
        ybsq_done = sem("ybsq_done")
        ybT_done = sem("ybT_done")
        ssqb_done = sem("ssqb_done")
        x1_done = sem("x1_done")
        h2_done = sem("h2_done")
        q_done = sem("q_done")
        qT_done = sem("qT_done")
        sc_done = sem("sc_done")
        best_done = sem("best_done")
        soft_done = sem("soft_done")
        idx_ready = sem("idx_ready")
        h2_ready = sem("h2_ready")
        xn_free = sem("xn_free")
        gat = [sem(f"gathered{r}") for r in range(RING)]
        dots = sem("dots")
        egelu = sem("egelu")
        diags = sem("diags")
        vdone = sem("vdone")
        y_taken = sem("y_taken")
        y_sq = sem("y_sq")
        y_ready = sem("y_ready")
        y_out = sem("y_out")
        v_out = sem("v_out")
        st_ready = sem("st_ready")
        st_out = sem("st_out")

        block = ctx.enter_context(nc.Block())

        def col(name, j=0, n=1):
            a = COLS[name][0] + j
            return par[:, a:a + n]

        def many(name, width):
            a, b = COLS[name]
            return par[:, a:b].unsqueeze(2).to_broadcast([P, b - a, width])

        uses = [len(range(r, SLOTS, RING)) for r in range(RING)]

        w_in_v = w_in.rearrange("(c p) n -> p c n", p=P)
        w_out_v = w_out.rearrange("(c p) n -> p c n", p=P)
        starts = [(w_in_v, c) for c in (512, 768, 0, 256, 1024, 1280, 1536, 1792)]
        starts += [(w_out_v, c) for c in (0, 256, 512, 768)]
        pieces = [w[:, :, c:c + PW] for w, c in starts]

        @block.sync
        def _(sp):
            def load_front(n):
                if n.offset or n.reg is not None:
                    sp.wait_ge(xn_free, n(1, 0))
                sp.dma_start(xn[:], x_all[bass.ds(n(P, 0), P), :]).then_inc(x_in, 16)

            def load_piece(n, k):
                if k >= 2 or n.offset or n.reg is not None:
                    sp.wait_ge(piece_done, n(PIECES, k - 1))
                sp.dma_start(wbuf[:, k % 2], pieces[k]).then_inc(w_in_s[k % 2], 16)

            def store_y(m):
                sp.wait_ge(y_ready, m(1, 1))
                sp.dma_start(y_all[bass.ds(m(P, 0), P), :], x1[:]).then_inc(y_out, 16)

            first = When(0)
            load_front(first)
            sp.dma_start(par[:], cols).then_inc(par_in, 16)
            load_piece(first, 0)
            load_piece(first, 1)
            for k in range(2, 8):
                load_piece(first, k)
            sp.wait_ge(v_done, 1)
            sp.dma_start(v_rows, vg[:]).then_inc(v_out, 16)
            for k in range(8, PIECES):
                load_piece(first, k)
            sp.dma_start(wq[:], w_q.rearrange("(c p) n -> p c n", p=P)).then_inc(wq_in, 16)
            sp.wait_ge(st_ready, 1)
            sp.dma_start(state_sample, last[:].rearrange("p m s -> p (m s)")).then_inc(st_out, 16)
            with sp.Fori(0, TILES - 1) as i:
                n, m = When(1, i), When(0, i)
                load_front(n)
                for k in range(PIECES):
                    load_piece(n, k)
                store_y(m)
            sp.wait_ge(st_ready, TILES)
            sp.dma_start(state_prompt, last[:].rearrange("p m s -> p (m s)")).then_inc(st_out, 16)
            store_y(When(TILES - 1))
            sp.wait_ge(v_out, 16)
            sp.wait_ge(st_out, 32)
            sp.wait_ge(y_out, 16 * TILES)

        @block.gpsimd
        def _(pool):
            nc.gpsimd.memset(eps[:], EPS).then_inc(eps_set, 1)
            nc.gpsimd.memset(ident[:], 0.0).then_inc(pool_set, 1)
            pool.wait_ge(pool_set, 1)
            nc.gpsimd.affine_select(out=ident[:], in_=ident[:], compare_op=ALU.not_equal, fill=1.0, base=0,
                                    pattern=[[-1, P]], channel_multiplier=1).then_inc(pool_set, 1)
            nc.gpsimd.iota(iota_i[:], [[1, TOPK]], 0, 0).then_inc(pool_set, 1)
            nc.gpsimd.memset(ones[:], 1.0).then_inc(pool_set, 1)
            nc.gpsimd.memset(ws_s, 0.0).then_inc(pool_set, 1)
            nc.gpsimd.memset(wab[:], 0.0).then_inc(pool_set, 1)
            nc.gpsimd.memset(wib[:], 0.0).then_inc(pool_set, 1)
            pool.dma_start(g_v[:], rows[0:1, 2 * D:2 * D + DH].to_broadcast([P, DH])).then_inc(rows_in, 16)
            pool.wait_ge(pool_set, 7)
            for b in range(NB):
                pool.dma_start(ws_s[b * NT:(b + 1) * NT, :, b * NT:(b + 1) * NT],
                               ws_t[0:NT, :, 0:NT]).then_inc(ws_in, 16)
            pool.wait_ge(ws_in, 16 * NB)
            nc.gpsimd.affine_select(out=ws_s, in_=ws_s, compare_op=ALU.is_ge, fill=0.0, base=0,
                                    pattern=[[0, GROUPS], [1, P]], channel_multiplier=-1).then_inc(pool_set, 1)
            pool.dma_start(xbuf[:].rearrange("p m (b s) -> p m b s", b=NB)[:, :, :, 0:HIST],
                           conv_state).then_inc(st_in, 16)
            pool.dma_start(carry[:], lru_state).then_inc(st_in, 16)
            for w, sbw in ((w_a, wab), (w_i, wib)):
                for e in range(2):
                    pool.dma_start(sbw[64 * e:64 * e + 64, :, 64 * e:64 * e + 64],
                                   w.rearrange("(m e) i j -> e i m j", e=2)[e]).then_inc(wab_in, 16)
            pool.dma_start(g_ffn[:], rows[0:1, 0:D].to_broadcast([P, D])).then_inc(rows_in, 16)
            pool.dma_start(keys[:], keys_t).then_inc(rows_in, 16)
            pool.dma_start(g_fin[:], rows[0:1, D:2 * D].to_broadcast([P, D])).then_inc(rows_in, 16)
            pool.dma_start(ws[:], ws_t).then_inc(wsp_in, 16)
            pool.wait_ge(wsp_in, 16)
            nc.gpsimd.affine_select(out=ws[:], in_=ws[:], compare_op=ALU.is_ge, fill=0.0, base=0,
                                    pattern=[[0, GROUPS], [1, P]], channel_multiplier=-1).then_inc(pool_set, 1)

            def gather_tile(m):
                for s in range(SLOTS):
                    if s % TOPK == 0:
                        pool.wait_ge(idx_ready, m(HEADS, s // TOPK + 1))
                        pool.sem_inc(pool_held, 1)
                    before = s - RING if s >= RING else s + (SLOTS - 1 - s) // RING * RING - SLOTS
                    pool.wait_ge(vdone, m(SLOTS, SLOTS + before + 1))
                    pool.sem_inc(pool_held, 1)
                    nc.gpsimd.indirect_dma_start(ring[:, s % RING], None, experts,
                                                 bass.IndirectOffsetOnAxis(ap=idc[:, s:s + 1], axis=0)
                                                 ).then_inc(gat[s % RING], 16)

            with pool.Fori(0, TILES) as i:
                gather_tile(When(0, i))

        @block.vector
        def _(v):
            st = Steps(v, dve_step, dve_held)
            V = nc.vector

            v.sem_inc(diags, SLOTS)
            v.sem_inc(y_taken, 2)
            v.wait_ge(par_in, 16)
            V.tensor_scalar(nbias[:], par[:, COLS["b_a"][0]:COLS["b_i"][1]], -1.0, None, ALU.mult).then_inc(dve_set, 1)
            V.tensor_scalar(lt[:, 0], col("lam", 0, HC), -1.0, None, ALU.mult).then_inc(dve_set, 1)
            v.wait_ge(dve_set, 2)
            V.tensor_tensor(lt[:, 1], lt[:, 0], col("lam", 0, HC), ALU.min).then_inc(dve_set, 1)
            v.wait_ge(act_set, 1)
            V.tensor_scalar(lt[:, 3], lt[:, 2], 2.0, None, ALU.add).then_inc(dve_set, 1)
            v.wait_ge(dve_set, 4)
            V.reciprocal(lt[:, 4], lt[:, 3]).then_inc(dve_set, 1)
            v.wait_ge(dve_set, 5)
            V.tensor_tensor(lt[:, 5], lt[:, 4], lt[:, 2], ALU.mult).then_inc(dve_set, 1)
            v.wait_ge(dve_set, 6)
            V.tensor_tensor(lt[:, 3], lt[:, 5], lt[:, 5], ALU.mult).then_inc(dve_set, 1)
            v.wait_ge(dve_set, 7)
            V.tensor_scalar(lt[:, 4], lt[:, 3], 1.0 / 17.0, None, ALU.mult).then_inc(dve_set, 1)
            done = 8
            for k in (15, 13, 11, 9, 7, 5, 3):
                v.wait_ge(dve_set, done)
                V.scalar_tensor_tensor(out=lt[:, 4], in0=lt[:, 4], scalar=1.0 / k, in1=lt[:, 3], op0=ALU.add,
                                       op1=ALU.mult).then_inc(dve_set, 1)
                done += 1
            v.wait_ge(dve_set, done)
            V.scalar_tensor_tensor(out=lt[:, 4], in0=lt[:, 4], scalar=1.0, in1=lt[:, 5], op0=ALU.add,
                                   op1=ALU.mult).then_inc(dve_set, 1)
            V.tensor_scalar(lt[:, 0], col("lam", 0, HC), 0.0, LRU_C, ALU.min, ALU.mult).then_inc(dve_set, 1)
            done += 2
            v.wait_ge(dve_set, done)
            V.scalar_tensor_tensor(out=lamc[:], in0=lt[:, 4], scalar=-2.0 * LRU_C, in1=lt[:, 0], op0=ALU.mult,
                                   op1=ALU.add).then_inc(dve_set, 1)
            v.wait_ge(pool_set, 3)
            V.tensor_copy(iota[:], iota_i[:]).then_inc(dve_set, 1)
            v.wait_ge(dve_set, done + 2)

            def rstd(n, j):
                st.step(V.reciprocal(rs[:, j:j + 1], rms[:, j:j + 1]), n)

            def front(p, n, sample):
                xs = xbuf[:].rearrange("p m (b s) -> p m b s", b=NB)

                def tap(m, k):
                    return xs[:, m, :, k:k + NT] if sample else xbuf[:, m, k:k + P]

                def seg(t):
                    return t.rearrange("p m (b s) -> p m b s", b=NB if sample else 1)

                if p == 1:
                    v.wait_ge(squares, n(NORMS, 2))
                    rstd(n, 0)
                    st.after()
                    st.gives(V.tensor_scalar(tmpA[:], xn[:], rs[:, 0:1], None, ALU.mult), h_done, n(1, 1))
                if p in (3, 35):
                    second = p == 35
                    v.wait_ge(turned, n(3, 3 if second else 1))
                    for b in range(2):
                        out = hT[:, 4 * b:4 * b + 4, :]
                        src = pt[:, b].rearrange("p (c t) -> p c t", c=4)
                        if second:
                            ins = V.tensor_copy(out, src)
                        else:
                            g = par[:, 4 * b:4 * b + 4].unsqueeze(2).to_broadcast([P, 4, P])
                            ins = V.tensor_tensor(out, src, g, ALU.mult)
                        if b == 0:
                            st.step(ins, n)
                        else:
                            st.gives(ins, hT_done, n(2, 2 if second else 1))
                if p == 7:
                    v.wait_ge(squares, n(NORMS, 4))
                    rstd(n, 1)
                    if sample:
                        v.wait_ge(rows_in, 64)
                    st.after()
                    st.gives(V.scalar_tensor_tensor(out=vg[:], in0=vg[:], scalar=rs[:, 1:2], in1=g_v[:], op0=ALU.mult,
                                                    op1=ALU.mult), v_done, n(1, 1))
                if p == 10:
                    v.wait_ge(spat_done, n(1, 1))
                    v.wait_ge(gelus, n(3, 2))
                    for g in range(GROUPS):
                        a = slice(g * P, g * P + P)
                        ins = V.scalar_tensor_tensor(out=ug[:, a], in0=ps[0][:, a],
                                                     scalar=col("bs_sample" if sample else "bs_prompt", g),
                                                     in1=ug[:, a], op0=ALU.add, op1=ALU.mult)
                        if g < GROUPS - 1:
                            st.step(ins, n)
                        else:
                            st.gives(ins, ya_done, n(1, 1))
                if p == 12:
                    v.wait_ge(turned, n(3, 2))
                    if sample:
                        v.wait_ge(v_out, 16)
                    st.gives(V.tensor_tensor(vg[:].rearrange("p (m t) -> p m t", m=HC),
                                             pt[:, 0].rearrange("p (c t) -> p c t", c=4), many("g_a", P), ALU.mult),
                             yaT_done, n(1, 1))
                if p == 13:
                    v.wait_ge(piece_done, n(PIECES, 6))
                    if sample:
                        v.wait_ge(st_in, 32)
                    for m in range(HC):
                        src = ps[2][:, m * P:(m + 1) * P]
                        out = xs[:, m, :, HIST:SEGS] if sample else xbuf[:, m, HIST:HIST + P]
                        if sample:
                            src = src.rearrange("p (b s) -> p b s", b=NB)
                        st.step(V.tensor_copy(out, src), n)
                if p in (13, 14):
                    for m in (0, 1) if p == 13 else (2, 3):
                        out = seg(xc[:])[:, m] if sample else xc[:, m]
                        st.after()
                        st.step(V.tensor_scalar(out, tap(m, 0), col("conv_w", m * TAPS), col("conv_b", m), ALU.mult,
                                                ALU.add), n)
                        for k in range(1, TAPS):
                            st.after()
                            ins = V.scalar_tensor_tensor(out=out, in0=tap(m, k), scalar=col("conv_w", m * TAPS + k),
                                                         in1=out, op0=ALU.mult, op1=ALU.add)
                            if (m, k) == (HC - 1, TAPS - 1):
                                st.gives(ins, xc_done, n(1, 1))
                            else:
                                st.step(ins, n)
                if p == 15:
                    st.after()
                    if sample:
                        st.step(V.tensor_copy(last[:, :, 0:NB * HIST].rearrange("p m (b k) -> p m b k", b=NB),
                                              xs[:, :, :, NT:SEGS]), n)
                        st.after()
                        st.step(V.memset(xbuf[:, :, 0:HIST], 0.0), n)
                    else:
                        st.step(V.tensor_copy(last[:, :, 0:HIST], xbuf[:, :, P:P + HIST]), n)
                        st.after()
                        st.step(V.tensor_copy(xbuf[:, :, 0:HIST], last[:, :, 0:HIST]), n)
                if p == 17:
                    v.wait_ge(exps_done, n(1, 1))
                    st.step(V.tensor_scalar(tmpA[:], tmpA[:], 1.0, None, ALU.add), n)
                    st.after()
                    st.gives(V.reciprocal(tmpA[:], tmpA[:]), rec_done, n(1, 1))
                th, a_t = tmpB[:, 0:DH], tmpB[:, DH:D]
                r_t, i_t = tmpA[:, 0:DH], tmpA[:, DH:D]
                if p == 18:
                    st.after()
                    st.step(V.tensor_tensor(i_t, i_t, xc[:].rearrange("p m t -> p (m t)"), ALU.mult), n)
                if p == 19:
                    v.wait_ge(decay_done, n(1, 1))
                    st.step(V.tensor_scalar(r_t, th, -1.0, 1.0, ALU.mult, ALU.add), n)
                    st.after()
                    st.step(V.reciprocal(r_t, r_t), n)
                    st.after()
                    st.gives(V.tensor_tensor(th, th, r_t, ALU.mult), growth_done, n(1, 1))
                if p == 21:
                    v.wait_ge(root_done, n(1, 1))
                    st.step(V.tensor_tensor(i_t, i_t, th, ALU.mult), n)
                if p == 21:
                    nb = NB if sample else 1
                    a4 = seg(a_t.rearrange("p (m t) -> p m t", m=HC))[:, :, :, 0]
                    b4 = seg(i_t.rearrange("p (m t) -> p m t", m=HC))[:, :, :, 0]
                    st.after()
                    st.step(V.tensor_tensor(cin[:, :, 0:nb], a4, carry[:, :, 0:nb], ALU.mult), n)
                    st.after()
                    st.step(V.tensor_tensor(b4, b4, cin[:, :, 0:nb], ALU.add), n)
                    st.after()
                    st.step(V.tensor_scalar(a4, a4, 0.0, None, ALU.mult), n)
                    for m in range(HC):
                        c = slice(m * P, m * P + P)
                        st.after()
                        st.step(V.tensor_tensor_scan(hl[:, m], a_t[:, c], i_t[:, c], 0.0, ALU.mult, ALU.add), n)
                if p == 22:
                    st.after()
                    if sample:
                        st.step(V.tensor_copy(last[:, :, NB * HIST:], seg(hl)[:, :, :, NT - 1]), n)
                        st.after()
                        st.gives(V.memset(carry[:, :, 0:1], 0.0), st_ready, n(1, 1))
                    else:
                        st.step(V.tensor_copy(carry[:, :, 0:1], hl[:, :, P - 1:P]), n)
                        st.after()
                        st.gives(V.tensor_copy(last[:, :, HIST:HIST + 1], carry[:, :, 0:1]), st_ready, n(1, 1))
                    st.after()
                    v.wait_ge(gelus, n(3, 3))
                    st.gives(V.tensor_tensor(hl, hl, gg[:], ALU.mult), yb_done, n(1, 1))
                if p == 23:
                    st.after()
                    st.gives(V.tensor_tensor(xc[:], hl, many("g_b", P), ALU.mult), ybT_done, n(1, 1))
                if p == 25:
                    v.wait_ge(squares, n(NORMS, 7))
                    rstd(n, 2)
                    rstd(n, 3)
                if p in (28, 31):
                    j = 0 if p == 28 else 1
                    v.wait_ge(piece_done, n(PIECES, 10 + 2 * j))
                    c = slice(j * 512, j * 512 + 512)
                    st.after()
                    st.step(V.scalar_tensor_tensor(out=xn[:, c], in0=ps[2 * j][:], scalar=rs[:, 2:3], in1=xn[:, c],
                                                   op0=ALU.mult, op1=ALU.add), n)
                    st.after()
                    ins = V.scalar_tensor_tensor(out=xn[:, c], in0=ps[2 * j + 1][:], scalar=rs[:, 3:4], in1=xn[:, c],
                                                 op0=ALU.mult, op1=ALU.add)
                    if j:
                        st.gives(ins, x1_done, n(1, 1))
                    else:
                        st.step(ins, n)
                if p == 33:
                    v.wait_ge(squares, n(NORMS, 9))
                    rstd(n, 4)
                    st.after()
                    st.gives(V.scalar_tensor_tensor(out=h2n[:], in0=xn[:], scalar=rs[:, 4:5], in1=g_ffn[:],
                                                    op0=ALU.mult, op1=ALU.mult), h2_done, n(1, 1))
                for r in range(4):
                    row = p - (40 + 5 * r)
                    if 0 <= row < 4:
                        half = row % 2
                        sc = ps[r][:, row * P:(row + 1) * P]
                        if row == 0:
                            v.wait_ge(sc_done, n(4, r + 1))
                        for t in range(2):
                            src = sc if t == 0 else srow
                            o = slice(8 * t, 8 * t + 8)
                            st.after_held()
                            st.step(V.max(vals[:, half, o], src), n)
                            st.after_held()
                            st.step(V.max_index(idx8[:, half, o], vals[:, half, o], src), n)
                            if t == 0:
                                st.after_held()
                                st.step(V.match_replace(srow, vals[:, half, o], sc, LOWEST), n)
                for h in range(HEADS):
                    if p == CHOOSE_AT[h]:
                        choose(h, n)
                    if p == CHOOSE_AT[h] + 1:
                        weights(h, n)

            def choose(h, n):
                top = best[:, h % 2]
                st.after()
                st.step(V.tensor_copy(idxf[:], idx8[:]), n)
                st.step(V.tensor_tensor(cand.rearrange("p (a b) -> p a b", a=TOPK),
                                        vals[:, 0].unsqueeze(2).to_broadcast([P, TOPK, TOPK]),
                                        vals[:, 1].unsqueeze(1).to_broadcast([P, TOPK, TOPK]), ALU.add), n)
                for t in range(2):
                    src = cand if t == 0 else left
                    o = slice(8 * t, 8 * t + 8)
                    st.after_held()
                    st.step(V.max(top[:, o], src), n)
                    st.after_held()
                    st.step(V.max_index(sel[:, o], top[:, o], src), n)
                    if t == 0:
                        st.after_held()
                        st.step(V.match_replace(left, top[:, o], cand, LOWEST), n)
                st.after()
                st.gives(V.tensor_scalar(nmax[:, h % 2:h % 2 + 1], top[:, 0:1], -1.0, None, ALU.mult), best_done,
                         n(HEADS, h + 1))
                st.step(V.tensor_scalar(selu[:, 0], sel[:], 4, None, ALU.logical_shift_right), n)
                st.step(V.tensor_scalar(selu[:, 1], sel[:], TOPK - 1, None, ALU.bitwise_and), n)
                st.after()
                st.step(V.tensor_copy(selfl[:], selu[:]), n)
                for half in range(2):
                    st.after()
                    st.step(V.tensor_tensor(eqm, selfl[:, half].unsqueeze(2).to_broadcast([P, TOPK, TOPK]),
                                            iota[:].unsqueeze(1).to_broadcast([P, TOPK, TOPK]), ALU.is_equal), n)
                    st.after()
                    st.step(V.tensor_tensor(eqm, eqm, idxf[:, half].unsqueeze(1).to_broadcast([P, TOPK, TOPK]),
                                            ALU.mult), n)
                    st.after()
                    st.step(V.tensor_reduce(e12[:, half], eqm, AX_X, ALU.add), n)
                st.after()
                st.gives(V.scalar_tensor_tensor(out=idc[:, h * TOPK:(h + 1) * TOPK], in0=e12[:, 0], scalar=float(P),
                                                in1=e12[:, 1], op0=ALU.mult, op1=ALU.add), idx_ready, n(HEADS, h + 1))

            def weights(h, n):
                v.wait_ge(soft_done, n(HEADS, h + 1))
                if n.offset or n.reg is not None:
                    v.wait_ge(diags, n(SLOTS, (h + 1) * TOPK))
                st.step(V.reciprocal(gsum[:, 2 + h % 2:3 + h % 2], gsum[:, h % 2:h % 2 + 1]), n)
                st.after()
                st.step(V.tensor_scalar(gc[:, h * TOPK:(h + 1) * TOPK], gexp[:, h % 2],
                                        gsum[:, 2 + h % 2:3 + h % 2], None, ALU.mult), n)

            def dot_pair(g, m):
                if g == 0:
                    v.wait_ge(h2_ready, m(1, 1))
                for s in (2 * g, 2 * g + 1):
                    v.wait_ge(gat[s % RING], m(16 * uses[s % RING], 16 * (s // RING + 1)))
                    if s % 2 == 0:
                        v.wait_ge(egelu, m(PAIRS, PAIRS + g - 3))
                    V.tensor_tensor_reduce(out=ring[:, s % RING, 0:D], in0=ring[:, s % RING, 0:D], in1=h2[:],
                                           scale=1.0, scalar=0.0, op0=ALU.mult, op1=ALU.add,
                                           accum_out=zt[:, s % 8:s % 8 + 1]).then_inc(dots, 1)

            def diag_pair(g, m):
                v.wait_ge(egelu, m(PAIRS, PAIRS + g + 1))
                for s in (2 * g, 2 * g + 1):
                    v.wait_ge(vdone, m(SLOTS, SLOTS + s - DIAGS + 1))
                    V.tensor_scalar(diag[:, s % DIAGS], ident[:], ge[:, s % 8:s % 8 + 1], gc[:, s:s + 1], ALU.mult,
                                    ALU.mult).then_inc(diags, 1)

            def adopt_h2(m):
                st.after()
                st.gives(V.tensor_copy(h2[:], h2n[:]), h2_ready, m(1, 1))

            def adopt_x(m):
                st.after()
                st.gives(V.tensor_copy(x1[:], xn[:]), xn_free, m(1, 1))

            def take_y(m):
                v.wait_ge(vdone, m(SLOTS, 2 * SLOTS))
                V.tensor_tensor(x1[:], x1[:], accY[:].rearrange("p a b -> p (a b)"), ALU.add).then_inc(y_taken, 1)

            def norm_y(m):
                v.wait_ge(y_sq, m(2, 2))
                V.reciprocal(yrms[:, 2:3], yrms[:, 1:2]).then_inc(y_taken, 1)
                v.wait_ge(y_taken, m(2, 4))
                V.scalar_tensor_tensor(out=x1[:], in0=x1[:], scalar=yrms[:, 2:3], in1=g_fin[:], op0=ALU.mult,
                                       op1=ALU.mult).then_inc(y_ready, 1)

            first = When(0)
            for p in range(STEPS):
                if p in EARLY:
                    dot_pair(EARLY[p], first)
                    diag_pair(EARLY[p], first)
                front(p, first, True)
                if p == 34:
                    adopt_h2(first)
            weights(HEADS - 1, first)
            adopt_x(first)
            per = st.count
            st.per = per
            with v.Fori(0, TILES - 1) as i:
                n, m = When(1, i), When(0, i)
                st.count, st.last = 0, (xn_free, n(1, 0))
                for g in range(LEAD, PAIRS):
                    dot_pair(g, m)
                    diag_pair(g, m)
                    front(g - LEAD, n, False)
                adopt_h2(n)
                for g in range(LEAD):
                    dot_pair(g, n)
                    if g == 0:
                        weights(HEADS - 1, n)
                        take_y(m)
                    if g == 2:
                        norm_y(m)
                    diag_pair(g, n)
                v.wait_ge(y_out, m(16, 16))
                adopt_x(n)
                assert st.count == per, (st.count, per)
            m = When(TILES - 1)
            for g in range(LEAD, PAIRS):
                dot_pair(g, m)
                diag_pair(g, m)
            take_y(m)
            norm_y(m)

        @block.scalar
        def _(a):
            st = Steps(a, act_step, act_held)
            A = nc.scalar

            a.sem_inc(egelu, PAIRS)
            a.wait_ge(eps_set, 1)
            a.wait_ge(dve_set, 3)
            A.activation(lt[:, 2], lt[:, 1], ACT.Exp).then_inc(act_set, 1)

            def mean_root(n, k, junk, src, j, width):
                A.activation(junk, src, ACT.Square, accum_out=ssq[:, j:j + 1]).then_inc(squares, 1)
                a.wait_ge(squares, n(NORMS, k))
                A.activation(rms[:, j:j + 1], ssq[:, j:j + 1], ACT.Sqrt, bias=eps[:, 0:1],
                             scale=1.0 / width).then_inc(squares, 1)

            def front(p, n):
                if p == 0:
                    a.wait_ge(x_in, n(16, 16))
                    mean_root(n, 1, tmpA[:], xn[:], 0, D)
                if p == 6:
                    a.wait_ge(piece_done, n(PIECES, 2))
                    A.activation(vg[:], ps[0][:], ACT.Gelu_apprx_tanh).then_inc(gelus, 1)
                    a.wait_ge(gelus, n(3, 1))
                    mean_root(n, 3, tmpB[:, 0:DH], vg[:], 1, DH)
                if p == 8:
                    a.wait_ge(piece_done, n(PIECES, 4))
                    A.activation(ug[:], ps[1][:], ACT.Gelu_apprx_tanh).then_inc(gelus, 1)
                if p == 11:
                    a.wait_ge(ya_done, n(1, 1))
                    mean_root(n, 5, tmpB[:, DH:D], ug[:], 2, DH)
                if p == 14:
                    a.wait_ge(piece_done, n(PIECES, 8))
                    A.activation(gg[:].rearrange("p m t -> p (m t)"), ps[3][:], ACT.Gelu_apprx_tanh).then_inc(gelus, 1)
                if p == 16:
                    a.wait_ge(gates_done, n(1, 1))
                    for j in range(2 * HC):
                        ins = A.activation(tmpA[:, j * P:(j + 1) * P], pt[:, j // HC, (j % HC) * P:(j % HC + 1) * P],
                                           ACT.Exp, bias=nbias[:, j:j + 1], scale=-1.0)
                    ins.then_inc(exps_done, 1)
                if p == 18:
                    a.wait_ge(rec_done, n(1, 1))
                    for f, o in ((ACT.Tanh, 0), (ACT.Exp, DH)):
                        for m in range(HC):
                            ins = A.activation(tmpB[:, o + m * P:o + (m + 1) * P], tmpA[:, m * P:(m + 1) * P], f,
                                               scale=lamc[:, m:m + 1])
                    ins.then_inc(decay_done, 1)
                if p == 23:
                    a.wait_ge(yb_done, n(1, 1))
                    A.activation(tmpA[:, 0:DH], hl.rearrange("p m t -> p (m t)"), ACT.Square).then_inc(ybsq_done, 1)
                if p == 20:
                    a.wait_ge(growth_done, n(1, 1))
                    A.activation(tmpB[:, 0:DH], tmpB[:, 0:DH], ACT.Sqrt, scale=-2.0).then_inc(root_done, 1)
                if p == 24:
                    a.wait_ge(ssqb_done, n(1, 1))
                    A.activation(rms[:, 3:4], pt[:, 1, 0:1], ACT.Sqrt, bias=eps[:, 0:1], scale=1.0 / DH
                                 ).then_inc(squares, 1)
                if p == 32:
                    a.wait_ge(x1_done, n(1, 1))
                    mean_root(n, 8, tmpB[:], xn[:], 4, D)
                for r in range(4):
                    if p == 38 + 5 * r:
                        a.wait_ge(q_done, n(4, r + 1))
                        if r >= 2:
                            a.wait_ge(sc_done, n(4, r - 1))
                        A.activation(qT[:, r % 2].rearrange("p q t -> p (q t)"), pt[:, r % 2], ACT.Copy
                                     ).then_inc(qT_done, 1)
                for h in range(HEADS):
                    if p == CHOOSE_AT[h]:
                        o = slice(h % 2, h % 2 + 1)
                        a.wait_ge(best_done, n(HEADS, h + 1))
                        A.activation(gexp[:, h % 2], best[:, h % 2], ACT.Exp, bias=nmax[:, o], accum_out=gsum[:, o]
                                     ).then_inc(soft_done, 1)

            def gelu_pair(g, m):
                a.wait_ge(dots, m(SLOTS, 2 * g + 2))
                o = 2 * g % 8
                a.wait_ge(diags, m(SLOTS, SLOTS + 2 * g - 6))
                A.activation(ge[:, o:o + 2], zt[:, o:o + 2], ACT.Gelu_apprx_tanh).then_inc(egelu, 1)

            def square_y(m):
                a.wait_ge(y_taken, m(2, 3))
                A.activation(tmpB[:], x1[:], ACT.Square, accum_out=yrms[:, 0:1]).then_inc(y_sq, 1)
                a.wait_ge(y_sq, m(2, 1))
                A.activation(yrms[:, 1:2], yrms[:, 0:1], ACT.Sqrt, bias=eps[:, 0:1], scale=1.0 / D
                             ).then_inc(y_sq, 1)

            first = When(0)
            for p in range(STEPS):
                if p in EARLY:
                    gelu_pair(EARLY[p], first)
                front(p, first)
            with a.Fori(0, TILES - 1) as i:
                n, m = When(1, i), When(0, i)
                for g in range(LEAD, PAIRS):
                    gelu_pair(g, m)
                    front(g - LEAD, n)
                for g in range(LEAD):
                    gelu_pair(g, n)
                    if g == 0:
                        square_y(m)
            m = When(TILES - 1)
            for g in range(LEAD, PAIRS):
                gelu_pair(g, m)
            square_y(m)

        @block.tensor
        def _(t):
            T = nc.tensor

            def piece(n, k):
                if k == 0:
                    t.wait_ge(hT_done, n(2, 1))
                if k == 8:
                    t.wait_ge(squares, n(NORMS, 7))
                    t.wait_ge(yaT_done, n(1, 1))
                t.wait_ge(w_in_s[k % 2], n(PIECES // 2 * 16, 16 * (k // 2 + 1)))
                w = wbuf[:, k % 2]
                half = slice((k % 2) * PW, (k % 2 + 1) * PW)
                if k < 4:
                    for c in range(DC):
                        ins = T.matmul(ps[k // 2][:, half], hT[:, c], w[:, c], start=c == 0, stop=c == DC - 1)
                elif k < 8:
                    for m in range(PW // P):
                        o = (k % 2) * PW + m * P
                        for c in range(DC):
                            ins = T.matmul(ps[k // 2][:, o:o + P], w[:, c, m * P:(m + 1) * P], hT[:, c],
                                           start=c == 0, stop=c == DC - 1)
                else:
                    j = (k - 8) // 2
                    for c in range(HC):
                        T.matmul(ps[2 * j][:, half], vg[:, c * P:(c + 1) * P], w[:, c], start=c == 0,
                                 stop=c == HC - 1)
                    for c in range(HC):
                        ins = T.matmul(ps[2 * j + 1][:, half], xc[:, c], w[:, HC + c], start=c == 0,
                                       stop=c == HC - 1)
                ins.then_inc(piece_done, 1)

            def front(p, n, sample):
                if p in (2, 34):
                    src = tmpA if p == 2 else h2n
                    if p == 2:
                        t.wait_ge(h_done, n(1, 1))
                    else:
                        t.wait_ge(h2_done, n(1, 1))
                    if p == 2 and sample:
                        t.wait_ge(pool_set, 2)
                    for c in range(DC):
                        ins = T.transpose(pt[:, c // 4, (c % 4) * P:(c % 4 + 1) * P], src[:, c * P:(c + 1) * P],
                                          ident[:])
                    ins.then_inc(turned, 1)
                for pos, k in ((4, 0), (5, 1), (6, 2), (7, 3), (10, 4), (11, 5), (12, 6), (13, 7), (26, 8), (27, 9),
                               (29, 10), (30, 11)):
                    if p == pos:
                        piece(n, k)
                if p == 9:
                    t.wait_ge(v_done, n(1, 1))
                    t.wait_ge(pool_set, 8 if sample else 9)
                    for g in range(GROUPS):
                        ins = T.matmul(ps[0][:, g * P:(g + 1) * P], (ws_s if sample else ws)[:, g],
                                       vg[:, g * P:(g + 1) * P], start=True, stop=True)
                    ins.then_inc(spat_done, 1)
                if p == 11:
                    t.wait_ge(ya_done, n(1, 1))
                    for c in range(HC):
                        ins = T.transpose(pt[:, 0, c * P:(c + 1) * P], ug[:, c * P:(c + 1) * P], ident[:])
                    ins.then_inc(turned, 1)
                if p == 15:
                    t.wait_ge(xc_done, n(1, 1))
                    if sample:
                        t.wait_ge(wab_in, 64)
                    for j, w in enumerate((wab, wib)):
                        for m in range(HC):
                            ins = T.matmul(pt[:, j, m * P:(m + 1) * P], w[:, m], xc[:, m], start=True, stop=True)
                    ins.then_inc(gates_done, 1)
                if p == 24:
                    t.wait_ge(ybsq_done, n(1, 1))
                    for c in range(HC):
                        ins = T.matmul(pt[:, 1, 0:1], tmpA[:, c * P:(c + 1) * P], ones[:, 0:1], start=c == 0,
                                       stop=c == HC - 1)
                    ins.then_inc(ssqb_done, 1)
                    t.wait_ge(ybT_done, n(1, 1))
                for r in range(4):
                    if p in (36 + 5 * r, 37 + 5 * r):
                        first = p == 36 + 5 * r
                        if r == 0 and first:
                            t.wait_ge(hT_done, n(2, 2))
                            if sample:
                                t.wait_ge(wq_in, 16)
                        if r >= 2 and first:
                            t.wait_ge(qT_done, n(4, r - 1))
                        for q in (0, 1) if first else (2, 3):
                            for c in range(DC):
                                ins = T.matmul(pt[:, r % 2, q * P:(q + 1) * P],
                                               wq[:, c, (4 * r + q) * P:(4 * r + q + 1) * P], hT[:, c],
                                               start=c == 0, stop=c == DC - 1)
                        if not first:
                            ins.then_inc(q_done, 1)
                    if p == 39 + 5 * r:
                        t.wait_ge(qT_done, n(4, r + 1))
                        if sample and r == 0:
                            t.wait_ge(rows_in, 64)
                        for q in range(4):
                            ins = T.matmul(ps[r][:, q * P:(q + 1) * P], qT[:, r % 2, q], keys[:, q % 2], start=True,
                                           stop=True)
                        ins.then_inc(sc_done, 1)

            def weigh_pair(g, m):
                if g == 0:
                    t.wait_ge(y_taken, m(2, 1))
                for s in (2 * g, 2 * g + 1):
                    t.wait_ge(diags, m(SLOTS, SLOTS + s + 1))
                    for j in range(2):
                        ins = T.matmul(accY[:, j], diag[:, s % DIAGS], ring[:, s % RING, D + j * 512:D + (j + 1) * 512],
                                       start=s == 0, stop=s == SLOTS - 1)
                    ins.then_inc(vdone, 1)

            t.sem_inc(vdone, SLOTS)
            first = When(0)
            for p in range(STEPS):
                if p in EARLY:
                    weigh_pair(EARLY[p], first)
                front(p, first, True)
            with t.Fori(0, TILES - 1) as i:
                n, m = When(1, i), When(0, i)
                for g in range(LEAD, PAIRS):
                    weigh_pair(g, m)
                    front(g - LEAD, n, False)
                for g in range(LEAD):
                    weigh_pair(g, n)
            m = When(TILES - 1)
            for g in range(LEAD, PAIRS):
                weigh_pair(g, m)


def kernel(**inputs):
    import numpy as np
    import concourse.bacc as bacc
    from concourse.bass_utils import run_bass_kernel_spmd

    a = {k: np.asarray(x) for k, x in inputs.items()}

    def by_channel(x):
        x = x.reshape(x.shape[:-1] + (x.shape[-1] // P, P))
        return np.moveaxis(x, (-1, -2), (0, 1)).reshape(P, -1)

    bs = a["b_s"][0].T
    cols = np.concatenate([
        by_channel(a["g_mix"][0]), by_channel(a["g_out_a"][0]), by_channel(a["g_out_b"][0]),
        by_channel(a["conv_w"][0]), by_channel(a["conv_b"][0]), by_channel(a["b_a"][0]), by_channel(a["b_i"][0]),
        by_channel(a["lam"][0]), bs, np.concatenate([bs[0:NT]] * NB, axis=0)], axis=1)
    feed = {
        "x_all": np.concatenate([a["x_sample"].reshape(NB * NT, D), a["x_prompt"].reshape(-1, D)], axis=0),
        "cols": cols,
        "conv_state": by_channel(a["state_conv"][0]).reshape(P, HC, NB, HIST),
        "lru_state": by_channel(a["state_lru"][0]).reshape(P, HC, NB),
        "w_in": a["w_in"][0], "w_out": a["w_out"][0], "w_q": a["w_q"][0],
        "ws_t": np.transpose(a["w_s"][0], (2, 0, 1)),
        "w_a": a["w_a"][0], "w_i": a["w_i"][0],
        "keys_t": np.stack([a["k_sub1"][0].T, a["k_sub2"][0].T], axis=1),
        "rows": np.concatenate([a["g_ffn"][0], a["g_final"], a["g_v"][0]])[None, :],
        "experts": np.concatenate([a["u_tab"][0], a["v_tab"][0]], axis=1),
    }
    feed = {k: np.ascontiguousarray(x) for k, x in feed.items()}
    nc = bacc.Bacc("TRN2", target_bir_lowering=False, num_devices=1)
    args = [nc.dram_tensor(k, x.shape, mybir.dt.from_np(x.dtype), kind="ExternalInput").ap() for k, x in feed.items()]
    outs = {"y_all": (TILES * P, D), "v_rows": (P, DH), "state_sample": (P, HC * NB * (HIST + 1)),
            "state_prompt": (P, HC * NB * (HIST + 1))}
    args += [nc.dram_tensor(k, s, F32, kind="ExternalOutput").ap() for k, s in outs.items()]
    hybrid_layer(nc, *args)
    got = run_bass_kernel_spmd(nc, [feed], core_ids=[0]).results[0]
    y = got["y_all"]
    ss = got["state_sample"].reshape(P, HC, NB * (HIST + 1))
    sp = got["state_prompt"].reshape(P, HC, NB * (HIST + 1))

    def channels(x):
        x = np.moveaxis(x, (1, 0), (-2, -1))
        return np.ascontiguousarray(x.reshape(x.shape[:-2] + (DH,)))

    conv_s = channels(ss[:, :, 0:NB * HIST].reshape(P, HC, NB, HIST))[None]
    lru_s = channels(ss[:, :, NB * HIST:])[None]
    conv_p = channels(sp[:, :, 0:HIST])[None, None]
    lru_p = channels(sp[:, :, HIST])[None, None]
    return (y[P:].reshape(1, -1, D), y[0:P].reshape(NB, NT, D), conv_p, lru_p, conv_s, lru_s,
            got["v_rows"].reshape(1, NB, NT, DH))
```

```python
from contextlib import ExitStack

import concourse.bass as bass
from concourse import mybir

F32 = mybir.dt.float32
I32 = mybir.dt.int32
U32 = mybir.dt.uint32
ALU = mybir.AluOpType
ACT = mybir.ActivationFunctionType
AX_X = mybir.AxisListType.X

P = 128
D = 1024
DC = D // P
DH = 512
HC = DH // P
GROUPS = 4
TILES = 5
NB, NT = 8, 16
TAPS = 4
HIST = TAPS - 1
SEGS = NT + HIST
HEADS = 8
TOPK = 16
SLOTS = HEADS * TOPK
RING = 6
SHORT = -SLOTS % RING
LONG = (SLOTS - SHORT * (RING - 1)) // RING
PLACE = [p for n in [RING] * LONG + [RING - 1] * SHORT for p in range(n)]
PAIRS = SLOTS // 2
LEAD = 12
STEPS = PAIRS - LEAD
EARLY = {p: g for g, p in enumerate([38] + list(range(40, 39 + LEAD)))}
ROUNDS = 4
PER_ROUND = SLOTS // ROUNDS
Q_AT = [27 + 5 * r for r in range(ROUNDS)]
DIAGS = 4
PW = 256
COLUMNS = [(0, 1024, P, 2), (0, 1024 + P, P, 2), (0, 1280, PW, 2), (0, 1536, PW, 3), (0, 1792, PW, 3),
           (0, 512, PW, 0), (0, 768, PW, 0), (0, 0, PW, 1), (0, 256, PW, 1),
           (1, 0, PW, 0), (1, 256, PW, 0), (1, 512, PW, 2), (1, 768, PW, 2)]
PIECES = len(COLUMNS)
KEPT = (3, 5, 7)
STREAMED = [k for k in range(PIECES) if k not in KEPT]
NORMS = 9
EPS = 1e-6
LOWEST = -3.0e38
LRU_C = 8.0

COLS = {}
_at = 0
for _name, _n in (("g_mix", DC), ("g_a", HC), ("g_b", HC), ("conv_w", HC * TAPS), ("conv_b", HC), ("b_a", HC),
                  ("b_i", HC), ("lam", HC), ("bs_prompt", GROUPS), ("bs_sample", GROUPS)):
    COLS[_name] = (_at, _at + _n)
    _at += _n
NCOLS = _at


class When:

    def __init__(self, offset, reg=None):
        self.offset, self.reg = offset, reg

    def __call__(self, per, k):
        fixed = self.offset * per + k
        return fixed if self.reg is None else self.reg * per + fixed


class Steps:

    def __init__(self, eng, own, held):
        self.eng, self.own, self.held = eng, own, held
        self.per, self.count, self.last = 0, 0, None

    def after(self):
        if self.last is not None:
            self.eng.wait_ge(*self.last)

    def need(self, product, held=False):
        self.eng.wait_ge(*product)
        if held:
            self.eng.sem_inc(self.held, 1)

    def step(self, ins, n):
        self.count += 1
        ins.then_inc(self.own, 1)
        self.last = (self.own, n(self.per, self.count))
        return self.last

    def gives(self, ins, sem, value):
        ins.then_inc(sem, 1)
        self.last = (sem, value)
        return self.last


def hybrid_layer(nc, x_all, cols, conv_state, lru_state, w_in, w_out, w_q, ws_t, w_a, w_i, keys_t, rows, experts,
                 y_all, v_rows, state_sample, state_prompt):
    with ExitStack() as ctx:
        def sb(name, shape, dt=F32):
            return ctx.enter_context(nc.sbuf_tensor(name, [P] + shape, dt))

        def sem(name):
            return ctx.enter_context(nc.semaphore(name))

        ring = sb("ring", [RING, 2 * D])
        wbuf = sb("wbuf", [2, DC, PW])
        wkept = sb("wkept", [len(KEPT), DC, PW])
        wq = sb("wq", [DC, 2 * HEADS * P])
        xn = sb("xn", [D])
        x1 = sb("x1", [D])
        h2 = sb("h2", [D])
        hT = sb("hT", [DC, P])
        tmpA = sb("tmpA", [D])
        tmpB = sb("tmpB", [D])
        vg = sb("vg", [DH])
        xbuf = sb("xbuf", [HC, NB * SEGS])
        xc = sb("xc", [HC, P])
        ya = tmpA[:, 0:DH]
        hl = tmpB[:, 0:DH].rearrange("p (m t) -> p m t", m=HC)
        g_ffn = sb("g_ffn", [D])
        g_fin = sb("g_fin", [D])
        g_v = sb("g_v", [DH])
        ws = sb("ws", [GROUPS, P])
        wab = sb("wab", [HC, P])
        wib = sb("wib", [HC, P])
        keys = sb("keys", [2, P])
        ident = sb("ident", [P])
        ones = sb("ones", [2])
        iota_i = sb("iota_i", [TOPK], I32)
        iota = sb("iota", [TOPK])
        par = sb("par", [NCOLS])
        nbias = sb("nbias", [2 * HC])
        lamc = sb("lamc", [HC])
        lt = sb("lt", [6, HC])
        carry = sb("carry", [HC, NB])
        cin = sb("cin", [HC, NB])
        last = sb("last", [HC, NB * (HIST + 1)])
        ssq = sb("ssq", [8])
        rms = sb("rms", [8])
        rs = sb("rs", [8])
        eps = sb("eps", [1])
        yrms = sb("yrms", [4])
        vals = sb("vals", [2, 2, TOPK])
        idx8 = sb("idx8", [2, 2, TOPK], U32)
        best = sb("best", [2, TOPK])
        sel = sb("sel", [2, TOPK], U32)
        selu = sb("selu", [2, 2, TOPK], U32)
        e12 = sb("e12", [2, 2, TOPK])
        nmax = sb("nmax", [2])
        gexp = sb("gexp", [2, TOPK])
        gsum = sb("gsum", [2, 2])
        gc = sb("gc", [SLOTS])
        idc = sb("idc", [SLOTS], I32)
        zt = sb("zt", [8])
        ge = sb("ge", [8])
        diag = sb("diag", [DIAGS, P])

        srow = tmpB[:, 0:2 * P].rearrange("p (e k) -> p e k", e=2)
        cand = tmpB[:, 0:512].rearrange("p (h k) -> p h k", h=2)
        left = tmpB[:, 512:1024].rearrange("p (h k) -> p h k", h=2)
        eqm = tmpB[:].rearrange("p (k a) -> p k a", a=TOPK)
        qT = tmpA[:].rearrange("p (b q t) -> p b q t", b=2, q=4)
        ws_s = ring[:, 0, 0:GROUPS * P].rearrange("p (g n) -> p g n", g=GROUPS)

        accY = ctx.enter_context(nc.psum_tensor("accY", [P, 2, 512], F32))
        ps = [ctx.enter_context(nc.psum_tensor(f"psF{i}", [P, 512], F32)) for i in range(4)]
        pt = ctx.enter_context(nc.psum_tensor("psT", [P, 2, 512], F32))

        par_in = sem("par_in")
        rows_in = sem("rows_in")
        gv_in = sem("gv_in")
        wq_in = [sem(f"wq_in{r}") for r in range(ROUNDS)]
        ws_in = sem("ws_in")
        wsp_in = sem("wsp_in")
        wab_in = sem("wab_in")
        st_in = sem("st_in")
        x_in = sem("x_in")
        streamed_in = [sem("streamed_in0"), sem("streamed_in1")]
        first_in = [sem(f"first_in{k}") for k in range(PIECES)]
        eps_set = sem("eps_set")
        pool_set = sem("pool_set")
        dve_set = sem("dve_set")
        act_set = sem("act_set")
        dve_step = sem("dve_step")
        dve_held = sem("dve_held")
        pool_held = sem("pool_held")
        squares = sem("squares")
        growth_done = sem("growth_done")
        root_done = sem("root_done")
        h_done = sem("h_done")
        turned = sem("turned")
        hT_done = sem("hT_done")
        piece_done = sem("piece_done")
        gelus = sem("gelus")
        v_done = sem("v_done")
        spat_done = sem("spat_done")
        ya_done = sem("ya_done")
        yaT_done = sem("yaT_done")
        xc_done = sem("xc_done")
        gates_done = sem("gates_done")
        exps_done = sem("exps_done")
        rec_done = sem("rec_done")
        decay_done = sem("decay_done")
        yb_done = sem("yb_done")
        ybsq_done = sem("ybsq_done")
        ybT_done = sem("ybT_done")
        ssqb_done = sem("ssqb_done")
        x1_done = sem("x1_done")
        h2_done = sem("h2_done")
        q_done = sem("q_done")
        qT_done = sem("qT_done")
        sc_done = sem("sc_done")
        best_done = sem("best_done")
        soft_done = sem("soft_done")
        idx_ready = sem("idx_ready")
        h2_ready = sem("h2_ready")
        xn_free = sem("xn_free")
        gat = [sem(f"gathered{r}") for r in range(RING)]
        dots = sem("dots")
        egelu = sem("egelu")
        diags = sem("diags")
        vdone = sem("vdone")
        y_taken = sem("y_taken")
        y_sq = sem("y_sq")
        y_ready = sem("y_ready")
        y_out = sem("y_out")
        v_out = sem("v_out")
        st_ready = sem("st_ready")
        st_out = sem("st_out")

        block = ctx.enter_context(nc.Block())

        def col(name, j=0, n=1):
            a = COLS[name][0] + j
            return par[:, a:a + n]

        def many(name, width):
            a, b = COLS[name]
            return par[:, a:b].unsqueeze(2).to_broadcast([P, b - a, width])

        uses = [PLACE.count(r) for r in range(RING)]

        w_in_v = w_in.rearrange("(c p) n -> p c n", p=P)
        w_out_v = w_out.rearrange("(c p) n -> p c n", p=P)
        pieces = [(w_out_v if out else w_in_v)[:, :, c:c + width] for out, c, width, _ in COLUMNS]

        places = [wbuf[:, 0], wbuf[:, 1]] + [ring[:, r].rearrange("p (c n) -> p c n", c=DC) for r in range(1, RING)]

        def first_place(k):
            if k in KEPT:
                return wkept[:, KEPT.index(k)]
            return places[STREAMED.index(k) % len(places)][:, :, 0:COLUMNS[k][2]]

        @block.sync
        def _(sp):
            def load_front(n):
                if n.offset or n.reg is not None:
                    sp.wait_ge(xn_free, n(1, 0))
                sp.dma_start(xn[:], x_all[bass.ds(n(P, 0), P), :]).then_inc(x_in, 16)

            def load_streamed(n, j):
                k = STREAMED[j]
                sp.wait_ge(piece_done, n(PIECES, STREAMED[j - 2] + 1 - (PIECES if j < 2 else 0)))
                sp.dma_start(wbuf[:, j % 2, :, 0:COLUMNS[k][2]], pieces[k]).then_inc(streamed_in[j % 2], 16)

            def load_first(k):
                j = STREAMED.index(k) - len(places) if k not in KEPT else -1
                if j >= 0:
                    sp.wait_ge(piece_done, STREAMED[j] + 1)
                sp.dma_start(first_place(k), pieces[k]).then_inc(first_in[k], 16)

            def load_queries(r):
                c = slice(r * 512, r * 512 + 512)
                sp.dma_start(wq[:, :, c], w_q.rearrange("(c p) n -> p c n", p=P)[:, :, c]).then_inc(wq_in[r], 16)

            def store_y(m):
                sp.wait_ge(y_ready, m(1, 1))
                sp.dma_start(y_all[bass.ds(m(P, 0), P), :], tmpB[:]).then_inc(y_out, 16)

            first = When(0)
            load_front(first)
            sp.dma_start(par[:], cols).then_inc(par_in, 16)
            for k in range(PIECES):
                load_first(k)
            load_queries(0)
            sp.wait_ge(v_done, 1)
            sp.dma_start(v_rows, vg[:]).then_inc(v_out, 16)
            for r in range(1, ROUNDS):
                load_queries(r)
            sp.wait_ge(st_ready, 1)
            sp.dma_start(state_sample, last[:].rearrange("p m s -> p (m s)")).then_inc(st_out, 16)
            with sp.Fori(0, TILES - 1) as i:
                n, m = When(1, i), When(0, i)
                load_streamed(n, 0)
                load_streamed(n, 1)
                load_front(n)
                for j in range(2, len(STREAMED)):
                    load_streamed(n, j)
                store_y(m)
            sp.wait_ge(st_ready, TILES)
            sp.dma_start(state_prompt, last[:].rearrange("p m s -> p (m s)")).then_inc(st_out, 16)
            store_y(When(TILES - 1))
            sp.wait_ge(v_out, 16)
            sp.wait_ge(st_out, 32)
            sp.wait_ge(y_out, 16 * TILES)

        @block.gpsimd
        def _(pool):
            nc.gpsimd.memset(eps[:], EPS).then_inc(eps_set, 1)
            nc.gpsimd.memset(ident[:], 0.0).then_inc(pool_set, 1)
            pool.wait_ge(pool_set, 1)
            nc.gpsimd.affine_select(out=ident[:], in_=ident[:], compare_op=ALU.not_equal, fill=1.0, base=0,
                                    pattern=[[-1, P]], channel_multiplier=1).then_inc(pool_set, 1)
            nc.gpsimd.iota(iota_i[:], [[1, TOPK]], 0, 0).then_inc(pool_set, 1)
            nc.gpsimd.memset(ones[:], 1.0).then_inc(pool_set, 1)
            nc.gpsimd.memset(ws_s, 0.0).then_inc(pool_set, 1)
            nc.gpsimd.memset(wab[:], 0.0).then_inc(pool_set, 1)
            nc.gpsimd.memset(wib[:], 0.0).then_inc(pool_set, 1)
            pool.wait_ge(pool_set, 5)
            for b in range(NB):
                pool.dma_start(ws_s[b * NT:(b + 1) * NT, :, b * NT:(b + 1) * NT],
                               ws_t[0:NT, :, 0:NT]).then_inc(ws_in, 16)
            pool.dma_start(g_ffn[:], rows[0:1, 0:D].to_broadcast([P, D])).then_inc(rows_in, 16)
            pool.dma_start(keys[:], keys_t).then_inc(rows_in, 16)
            pool.dma_start(g_fin[:], rows[0:1, D:2 * D].to_broadcast([P, D])).then_inc(rows_in, 16)
            pool.dma_start(ws[:], ws_t).then_inc(wsp_in, 16)
            for spatial, loaded, count in ((ws_s, ws_in, 16 * NB), (ws[:], wsp_in, 16)):
                pool.wait_ge(loaded, count)
                nc.gpsimd.affine_select(out=spatial, in_=spatial, compare_op=ALU.is_ge, fill=0.0, base=0,
                                        pattern=[[0, GROUPS], [1, P]], channel_multiplier=-1).then_inc(pool_set, 1)

            def gather_tile(m):
                for s in range(SLOTS):
                    if s % PER_ROUND == 0:
                        pool.wait_ge(idx_ready, m(ROUNDS, s // PER_ROUND + 1))
                        pool.sem_inc(pool_held, 1)
                    before = [b - SLOTS for b in range(SLOTS) if PLACE[b] == PLACE[s]]
                    before = ([b for b in range(s) if PLACE[b] == PLACE[s]] or before)[-1]
                    pool.wait_ge(vdone, m(SLOTS, SLOTS + before + 1))
                    pool.sem_inc(pool_held, 1)
                    nc.gpsimd.indirect_dma_start(ring[:, PLACE[s]], None, experts,
                                                 bass.IndirectOffsetOnAxis(ap=idc[:, s:s + 1], axis=0)
                                                 ).then_inc(gat[PLACE[s]], 16)

            with pool.Fori(0, TILES) as i:
                gather_tile(When(0, i))

        @block.vector
        def _(v):
            st = Steps(v, dve_step, dve_held)
            V = nc.vector

            v.sem_inc(diags, SLOTS)
            v.sem_inc(y_taken, 2)
            v.wait_ge(par_in, 16)
            V.tensor_scalar(nbias[:], par[:, COLS["b_a"][0]:COLS["b_i"][1]], -1.0, None, ALU.mult).then_inc(dve_set, 1)
            V.tensor_scalar(lt[:, 0], col("lam", 0, HC), -1.0, None, ALU.mult).then_inc(dve_set, 1)
            v.wait_ge(dve_set, 2)
            V.tensor_tensor(lt[:, 1], lt[:, 0], col("lam", 0, HC), ALU.min).then_inc(dve_set, 1)
            v.wait_ge(act_set, 1)
            V.tensor_scalar(lt[:, 3], lt[:, 2], 2.0, None, ALU.add).then_inc(dve_set, 1)
            v.wait_ge(dve_set, 4)
            V.reciprocal(lt[:, 4], lt[:, 3]).then_inc(dve_set, 1)
            v.wait_ge(dve_set, 5)
            V.tensor_tensor(lt[:, 5], lt[:, 4], lt[:, 2], ALU.mult).then_inc(dve_set, 1)
            v.wait_ge(dve_set, 6)
            V.tensor_tensor(lt[:, 3], lt[:, 5], lt[:, 5], ALU.mult).then_inc(dve_set, 1)
            v.wait_ge(dve_set, 7)
            V.tensor_scalar(lt[:, 4], lt[:, 3], 1.0 / 17.0, None, ALU.mult).then_inc(dve_set, 1)
            done = 8
            for k in (15, 13, 11, 9, 7, 5, 3):
                v.wait_ge(dve_set, done)
                V.scalar_tensor_tensor(out=lt[:, 4], in0=lt[:, 4], scalar=1.0 / k, in1=lt[:, 3], op0=ALU.add,
                                       op1=ALU.mult).then_inc(dve_set, 1)
                done += 1
            v.wait_ge(dve_set, done)
            V.scalar_tensor_tensor(out=lt[:, 4], in0=lt[:, 4], scalar=1.0, in1=lt[:, 5], op0=ALU.add,
                                   op1=ALU.mult).then_inc(dve_set, 1)
            V.tensor_scalar(lt[:, 0], col("lam", 0, HC), 0.0, LRU_C, ALU.min, ALU.mult).then_inc(dve_set, 1)
            done += 2
            v.wait_ge(dve_set, done)
            V.scalar_tensor_tensor(out=lamc[:], in0=lt[:, 4], scalar=-2.0 * LRU_C, in1=lt[:, 0], op0=ALU.mult,
                                   op1=ALU.add).then_inc(dve_set, 1)
            v.wait_ge(pool_set, 3)
            V.tensor_copy(iota[:], iota_i[:]).then_inc(dve_set, 1)
            v.wait_ge(dve_set, done + 2)

            def rstd(n, j):
                st.step(V.reciprocal(rs[:, j:j + 1], rms[:, j:j + 1]), n)

            conv = [None] * HC
            scanned = [None]

            def front(p, n, sample):
                xs = xbuf[:].rearrange("p m (b s) -> p m b s", b=NB)

                def tap(m, k):
                    return xs[:, m, :, k:k + NT] if sample else xbuf[:, m, k:k + P]

                def seg(t):
                    return t.rearrange("p m (b s) -> p m b s", b=NB if sample else 1)

                if p == 1:
                    v.wait_ge(squares, n(NORMS, 2))
                    rstd(n, 0)
                    st.after()
                    st.gives(V.tensor_scalar(tmpA[:], xn[:], rs[:, 0:1], None, ALU.mult), h_done, n(1, 1))
                if p in (3, 26):
                    second = p == 26
                    v.wait_ge(turned, n(3, 3 if second else 1))
                    for b in range(2):
                        out = hT[:, 4 * b:4 * b + 4, :]
                        src = pt[:, b].rearrange("p (c t) -> p c t", c=4)
                        if second:
                            ins = V.tensor_copy(out, src)
                        else:
                            g = par[:, 4 * b:4 * b + 4].unsqueeze(2).to_broadcast([P, 4, P])
                            ins = V.tensor_tensor(out, src, g, ALU.mult)
                        if b == 0:
                            st.step(ins, n)
                        else:
                            st.gives(ins, hT_done, n(2, 2 if second else 1))
                if p == 11:
                    v.wait_ge(squares, n(NORMS, 4))
                    rstd(n, 1)
                    if sample:
                        v.wait_ge(gv_in, 16)
                    st.after()
                    st.gives(V.scalar_tensor_tensor(out=vg[:], in0=vg[:], scalar=rs[:, 1:2], in1=g_v[:], op0=ALU.mult,
                                                    op1=ALU.mult), v_done, n(1, 1))
                if p == 6:
                    v.wait_ge(piece_done, n(PIECES, 3))
                    if sample:
                        v.wait_ge(st_in, 32)
                    for m in range(HC):
                        src = ps[2][:, m * P:(m + 1) * P]
                        out = xs[:, m, :, HIST:SEGS] if sample else xbuf[:, m, HIST:HIST + P]
                        if sample:
                            src = src.rearrange("p (b s) -> p b s", b=NB)
                        st.step(V.tensor_copy(out, src), n)
                if p in (6, 7):
                    st.after()
                    for k in (0, 1) if p == 6 else (2, 3):
                        for m in range(HC):
                            out = seg(xc[:])[:, m] if sample else xc[:, m]
                            if k == 0:
                                ins = V.tensor_scalar(out, tap(m, 0), col("conv_w", m * TAPS), col("conv_b", m),
                                                      ALU.mult, ALU.add)
                            else:
                                if k != 2:
                                    st.need(conv[m])
                                ins = V.scalar_tensor_tensor(out=out, in0=tap(m, k), scalar=col("conv_w", m * TAPS + k),
                                                             in1=out, op0=ALU.mult, op1=ALU.add)
                            if (m, k) == (HC - 1, TAPS - 1):
                                st.gives(ins, xc_done, n(1, 1))
                            else:
                                conv[m] = st.step(ins, n)
                if p == 8:
                    st.after()
                    if sample:
                        st.step(V.tensor_copy(last[:, :, 0:NB * HIST].rearrange("p m (b k) -> p m b k", b=NB),
                                              xs[:, :, :, NT:SEGS]), n)
                        st.after()
                        st.step(V.memset(xbuf[:, :, 0:HIST], 0.0), n)
                    else:
                        st.step(V.tensor_copy(last[:, :, 0:HIST], xbuf[:, :, P:P + HIST]), n)
                        st.after()
                        st.step(V.tensor_copy(xbuf[:, :, 0:HIST], last[:, :, 0:HIST]), n)
                th, a_t = tmpB[:, 0:DH], tmpB[:, DH:D]
                r_t, i_t = tmpA[:, 0:DH], tmpA[:, DH:D]
                if p == 10:
                    v.wait_ge(exps_done, n(1, 1))
                    st.step(V.tensor_scalar(tmpA[:], tmpA[:], 1.0, None, ALU.add), n)
                    st.after()
                    st.gives(V.reciprocal(r_t, r_t), rec_done, n(1, 1))
                    st.step(V.reciprocal(i_t, i_t), n)
                if p == 11:
                    st.after()
                    st.step(V.tensor_tensor(i_t, i_t, xc[:].rearrange("p m t -> p (m t)"), ALU.mult), n)
                if p == 12:
                    v.wait_ge(decay_done, n(1, 1))
                    st.step(V.tensor_scalar(r_t, th, -1.0, 1.0, ALU.mult, ALU.add), n)
                    st.after()
                    st.step(V.reciprocal(r_t, r_t), n)
                    st.after()
                    st.gives(V.tensor_tensor(th, th, r_t, ALU.mult), growth_done, n(1, 1))
                if p == 13:
                    v.wait_ge(spat_done, n(1, 1))
                    v.wait_ge(gelus, n(3, 3))
                    for g in range(GROUPS):
                        a = slice(g * P, g * P + P)
                        ins = V.scalar_tensor_tensor(out=ya[:, a], in0=ps[0][:, a],
                                                     scalar=col("bs_sample" if sample else "bs_prompt", g),
                                                     in1=ya[:, a], op0=ALU.add, op1=ALU.mult)
                        if g < GROUPS - 1:
                            st.step(ins, n)
                        else:
                            st.gives(ins, ya_done, n(1, 1))
                if p == 14:
                    v.wait_ge(root_done, n(1, 1))
                    st.step(V.tensor_tensor(i_t, i_t, th, ALU.mult), n)
                    nb = NB if sample else 1
                    a4 = seg(a_t.rearrange("p (m t) -> p m t", m=HC))[:, :, :, 0]
                    b4 = seg(i_t.rearrange("p (m t) -> p m t", m=HC))[:, :, :, 0]
                    st.after()
                    st.step(V.tensor_tensor(cin[:, :, 0:nb], a4, carry[:, :, 0:nb], ALU.mult), n)
                    st.after()
                    st.step(V.tensor_tensor(b4, b4, cin[:, :, 0:nb], ALU.add), n)
                    st.after()
                    st.step(V.tensor_scalar(a4, a4, 0.0, None, ALU.mult), n)
                    for m in range(HC):
                        c = slice(m * P, m * P + P)
                        if m == 0:
                            st.after()
                        scanned[0] = st.step(V.tensor_tensor_scan(hl[:, m], a_t[:, c], i_t[:, c], 0.0, ALU.mult,
                                                                  ALU.add), n)
                if p == 15:
                    v.wait_ge(turned, n(3, 2))
                    if sample:
                        v.wait_ge(v_out, 16)
                    st.gives(V.tensor_tensor(vg[:].rearrange("p (m t) -> p m t", m=HC),
                                             pt[:, 0].rearrange("p (c t) -> p c t", c=4), many("g_a", P), ALU.mult),
                             yaT_done, n(1, 1))
                if p == 15:
                    v.wait_ge(*scanned[0])
                    if sample:
                        st.step(V.tensor_copy(last[:, :, NB * HIST:], seg(hl)[:, :, :, NT - 1]), n)
                        st.after()
                        st.gives(V.memset(carry[:, :, 0:1], 0.0), st_ready, n(1, 1))
                    else:
                        st.step(V.tensor_copy(carry[:, :, 0:1], hl[:, :, P - 1:P]), n)
                        st.after()
                        st.gives(V.tensor_copy(last[:, :, HIST:HIST + 1], carry[:, :, 0:1]), st_ready, n(1, 1))
                    st.after()
                    v.wait_ge(gelus, n(3, 1))
                    st.gives(V.tensor_tensor(hl, hl, ps[3][:].rearrange("p (m t) -> p m t", m=HC), ALU.mult),
                             yb_done, n(1, 1))
                if p == 16:
                    st.after()
                    st.gives(V.tensor_tensor(xc[:], hl, many("g_b", P), ALU.mult), ybT_done, n(1, 1))
                if p == 19:
                    v.wait_ge(squares, n(NORMS, 7))
                    rstd(n, 2)
                    rstd(n, 3)
                if p in (20, 22):
                    j = 0 if p == 20 else 1
                    v.wait_ge(piece_done, n(PIECES, 11 + 2 * j))
                    c = slice(j * 512, j * 512 + 512)
                    st.after()
                    st.step(V.scalar_tensor_tensor(out=xn[:, c], in0=ps[2 * j][:], scalar=rs[:, 2:3], in1=xn[:, c],
                                                   op0=ALU.mult, op1=ALU.add), n)
                    st.after()
                    ins = V.scalar_tensor_tensor(out=xn[:, c], in0=ps[2 * j + 1][:], scalar=rs[:, 3:4], in1=xn[:, c],
                                                 op0=ALU.mult, op1=ALU.add)
                    if j:
                        st.gives(ins, x1_done, n(1, 1))
                    else:
                        st.step(ins, n)
                if p == 24:
                    if sample:
                        v.wait_ge(rows_in, 48)
                    v.wait_ge(squares, n(NORMS, 9))
                    rstd(n, 4)
                    st.after()
                    st.gives(V.scalar_tensor_tensor(out=tmpB[:], in0=xn[:], scalar=rs[:, 4:5], in1=g_ffn[:],
                                                    op0=ALU.mult, op1=ALU.mult), h2_done, n(1, 1))
                for r in range(ROUNDS):
                    at = p - Q_AT[r]
                    if at == 9:
                        pick_numbers(r, n)
                        if r < ROUNDS - 1:
                            weights(r, n)
                    if at == 5:
                        v.wait_ge(sc_done, n(ROUNDS, r + 1))
                    if at in (5, 6):
                        best_keys(r, at - 5, n)
                    if at == 7:
                        best_sums(n)
                    if at == 8:
                        next_sums(r, n)

            def top_eight(t, srcs, outs, idxs, lefts, after, n):
                o = slice(8 * t, 8 * t + 8)
                made = []
                for e in range(2):
                    st.need(after[e], True)
                    made.append(st.step(V.max(outs[e][:, o], srcs[e]), n))
                for e in range(2):
                    st.need(made[e], True)
                    made[e] = st.step(V.max_index(idxs[e][:, o], outs[e][:, o], srcs[e]), n)
                if t == 0:
                    for e in range(2):
                        made[e] = st.step(V.match_replace(lefts[e], outs[e][:, o], srcs[e], LOWEST), n)
                return made

            def best_keys(r, h, n):
                srcs = [ps[r][:, (2 * h + e) * P:(2 * h + e + 1) * P] for e in range(2)]
                lefts = [srow[:, e] for e in range(2)]
                outs, idxs = [vals[:, h, e] for e in range(2)], [idx8[:, h, e] for e in range(2)]
                made = top_eight(0, srcs, outs, idxs, lefts, [st.last, st.last], n)
                top_eight(1, lefts, outs, idxs, None, made, n)

            def best_sums(n):
                st.after()
                made = [st.step(V.tensor_tensor(cand[:, h].rearrange("p (a b) -> p a b", a=TOPK),
                                                vals[:, h, 0].unsqueeze(2).to_broadcast([P, TOPK, TOPK]),
                                                vals[:, h, 1].unsqueeze(1).to_broadcast([P, TOPK, TOPK]), ALU.add), n)
                        for h in range(2)]
                top_eight(0, [cand[:, 0], cand[:, 1]], [best[:, 0], best[:, 1]], [sel[:, 0], sel[:, 1]],
                          [left[:, 0], left[:, 1]], made, n)

            def next_sums(r, n):
                top_eight(1, [left[:, 0], left[:, 1]], [best[:, 0], best[:, 1]], [sel[:, 0], sel[:, 1]], None,
                          [st.last, st.last], n)
                guard = st.gives(V.tensor_scalar(nmax[:], best[:, :, 0], -1.0, None, ALU.mult), best_done,
                                 n(ROUNDS, r + 1))
                st.need(guard)
                st.step(V.tensor_scalar(selu[:, :, 0], sel[:], 4, None, ALU.logical_shift_right), n)
                st.step(V.tensor_scalar(selu[:, :, 1], sel[:], TOPK - 1, None, ALU.bitwise_and), n)
                st.after()
                st.step(V.tensor_tensor(eqm, selu[:].rearrange("p h e k -> p (h e k)").unsqueeze(2).to_broadcast(
                    [P, 4 * TOPK, TOPK]), iota[:].unsqueeze(1).to_broadcast([P, 4 * TOPK, TOPK]), ALU.is_equal), n)

            def pick_numbers(r, n):
                eq4 = eqm.rearrange("p (q k) a -> p q k a", q=4)
                st.after()
                st.step(V.tensor_tensor(eq4, eq4, idx8[:].rearrange("p h e a -> p (h e) a").unsqueeze(2).to_broadcast(
                    [P, 4, TOPK, TOPK]), ALU.mult), n)
                st.after()
                st.step(V.tensor_reduce(e12[:].rearrange("p h e k -> p (h e k)"), eqm, AX_X, ALU.add), n)
                st.after()
                st.gives(V.scalar_tensor_tensor(
                    out=idc[:, r * PER_ROUND:(r + 1) * PER_ROUND].rearrange("p (h k) -> p h k", h=2), in0=e12[:, :, 0],
                    scalar=float(P), in1=e12[:, :, 1], op0=ALU.mult, op1=ALU.add), idx_ready, n(ROUNDS, r + 1))

            def weights(r, n):
                v.wait_ge(soft_done, n(HEADS, 2 * r + 2))
                if n.offset or n.reg is not None:
                    v.wait_ge(diags, n(SLOTS, (r + 1) * PER_ROUND))
                st.step(V.reciprocal(gsum[:, 1], gsum[:, 0]), n)
                st.after()
                st.step(V.tensor_tensor(gc[:, r * PER_ROUND:(r + 1) * PER_ROUND].rearrange("p (h k) -> p h k", h=2),
                                        gexp[:], gsum[:, 1].unsqueeze(2).to_broadcast([P, 2, TOPK]), ALU.mult), n)

            def dot(s, m):
                if s == 0:
                    v.wait_ge(h2_ready, m(1, 1))
                v.wait_ge(gat[PLACE[s]], m(16 * uses[PLACE[s]], 16 * (PLACE[:s].count(PLACE[s]) + 1)))
                v.wait_ge(egelu, m(SLOTS, SLOTS + s - 7))
                V.tensor_tensor_reduce(out=ring[:, PLACE[s], 0:D], in0=ring[:, PLACE[s], 0:D], in1=h2[:], scale=1.0,
                                       scalar=0.0, op0=ALU.mult, op1=ALU.add, accum_out=zt[:, s % 8:s % 8 + 1]
                                       ).then_inc(dots, 1)

            def weight(s, m):
                v.wait_ge(egelu, m(SLOTS, SLOTS + s + 1))
                v.wait_ge(vdone, m(SLOTS, SLOTS + s - DIAGS + 1))
                V.tensor_scalar(diag[:, s % DIAGS], ident[:], ge[:, s % 8:s % 8 + 1], gc[:, s:s + 1], ALU.mult,
                                ALU.mult).then_inc(diags, 1)

            def adopt_h2(m):
                st.after()
                st.gives(V.scalar_tensor_tensor(out=h2[:], in0=xn[:], scalar=rs[:, 4:5], in1=g_ffn[:], op0=ALU.mult,
                                                op1=ALU.mult), h2_ready, m(1, 1))

            def adopt_x(m):
                st.after()
                st.gives(V.tensor_copy(x1[:], xn[:]), xn_free, m(1, 1))

            def take_y(m):
                v.wait_ge(vdone, m(SLOTS, 2 * SLOTS))
                V.tensor_tensor(tmpB[:], x1[:], accY[:].rearrange("p a b -> p (a b)"), ALU.add).then_inc(y_taken, 1)

            def norm_y(m):
                v.wait_ge(y_sq, m(2, 2))
                V.reciprocal(yrms[:, 2:3], yrms[:, 1:2]).then_inc(y_taken, 1)
                v.wait_ge(y_taken, m(2, 4))
                V.scalar_tensor_tensor(out=tmpB[:], in0=tmpB[:], scalar=yrms[:, 2:3], in1=g_fin[:], op0=ALU.mult,
                                       op1=ALU.mult).then_inc(y_ready, 1)

            first = When(0)
            for p in range(STEPS):
                if p in EARLY:
                    dot(2 * EARLY[p], first)
                    dot(2 * EARLY[p] + 1, first)
                    weight(2 * EARLY[p], first)
                front(p, first, True)
                if p in EARLY:
                    weight(2 * EARLY[p] + 1, first)
                if p == 25:
                    adopt_h2(first)
                    adopt_x(first)
            weights(ROUNDS - 1, first)
            per = st.count
            st.per = per
            with v.Fori(0, TILES - 1) as i:
                n, m = When(1, i), When(0, i)
                st.count, st.last = 0, (xn_free, n(1, 0))
                for g in range(LEAD, PAIRS):
                    dot(2 * g, m)
                    dot(2 * g + 1, m)
                    weight(2 * g, m)
                    front(g - LEAD, n, False)
                    weight(2 * g + 1, m)
                adopt_h2(n)
                for g in range(LEAD):
                    dot(2 * g, n)
                    dot(2 * g + 1, n)
                    if g == 0:
                        weights(ROUNDS - 1, n)
                        take_y(m)
                    if g == 2:
                        norm_y(m)
                    weight(2 * g, n)
                    weight(2 * g + 1, n)
                    if g == 8:
                        adopt_x(n)
                v.wait_ge(y_out, m(16, 16))
                assert st.count == per, (st.count, per)
            m = When(TILES - 1)
            for g in range(LEAD, PAIRS):
                dot(2 * g, m)
                dot(2 * g + 1, m)
                weight(2 * g, m)
                weight(2 * g + 1, m)
            take_y(m)
            norm_y(m)

        @block.scalar
        def _(a):
            A = nc.scalar

            a.sem_inc(egelu, SLOTS)
            a.dma_start(xbuf[:].rearrange("p m (b s) -> p m b s", b=NB)[:, :, :, 0:HIST], conv_state
                        ).then_inc(st_in, 16)
            a.dma_start(carry[:], lru_state).then_inc(st_in, 16)
            a.wait_ge(pool_set, 7)
            for w, sbw in ((w_a, wab), (w_i, wib)):
                for e in range(2):
                    a.dma_start(sbw[64 * e:64 * e + 64, :, 64 * e:64 * e + 64],
                                w.rearrange("(m e) i j -> e i m j", e=2)[e]).then_inc(wab_in, 16)
            a.dma_start(g_v[:], rows[0:1, 2 * D:2 * D + DH].to_broadcast([P, DH])).then_inc(gv_in, 16)
            a.wait_ge(eps_set, 1)
            a.wait_ge(dve_set, 3)
            A.activation(lt[:, 2], lt[:, 1], ACT.Exp).then_inc(act_set, 1)

            def mean_root(n, k, junk, src, j, width):
                A.activation(junk, src, ACT.Square, accum_out=ssq[:, j:j + 1]).then_inc(squares, 1)
                a.wait_ge(squares, n(NORMS, k))
                A.activation(rms[:, j:j + 1], ssq[:, j:j + 1], ACT.Sqrt, bias=eps[:, 0:1],
                             scale=1.0 / width).then_inc(squares, 1)

            def front(p, n):
                if p == 0:
                    a.wait_ge(x_in, n(16, 16))
                    mean_root(n, 1, tmpA[:], xn[:], 0, D)
                if p == 8:
                    a.wait_ge(piece_done, n(PIECES, 5))
                    A.activation(ps[3][:], ps[3][:], ACT.Gelu_apprx_tanh).then_inc(gelus, 1)
                if p == 9:
                    a.wait_ge(gates_done, n(1, 1))
                    for j in range(2 * HC):
                        ins = A.activation(tmpA[:, j * P:(j + 1) * P], pt[:, j // HC, (j % HC) * P:(j % HC + 1) * P],
                                           ACT.Exp, bias=nbias[:, j:j + 1], scale=-1.0)
                    ins.then_inc(exps_done, 1)
                if p == 10:
                    a.wait_ge(piece_done, n(PIECES, 7))
                    A.activation(vg[:], ps[0][:], ACT.Gelu_apprx_tanh).then_inc(gelus, 1)
                    a.wait_ge(gelus, n(3, 2))
                    mean_root(n, 3, tmpB[:, 0:DH], vg[:], 1, DH)
                if p == 11:
                    a.wait_ge(rec_done, n(1, 1))
                    for f, o in ((ACT.Tanh, 0), (ACT.Exp, DH)):
                        for m in range(HC):
                            ins = A.activation(tmpB[:, o + m * P:o + (m + 1) * P], tmpA[:, m * P:(m + 1) * P], f,
                                               scale=lamc[:, m:m + 1])
                    ins.then_inc(decay_done, 1)
                if p == 13:
                    a.wait_ge(growth_done, n(1, 1))
                    a.wait_ge(piece_done, n(PIECES, 9))
                    A.activation(ya, ps[1][:], ACT.Gelu_apprx_tanh).then_inc(gelus, 1)
                    A.activation(tmpB[:, 0:DH], tmpB[:, 0:DH], ACT.Sqrt, scale=-2.0).then_inc(root_done, 1)
                if p == 14:
                    a.wait_ge(ya_done, n(1, 1))
                    mean_root(n, 5, ps[0][:], ya, 2, DH)
                if p == 16:
                    a.wait_ge(yb_done, n(1, 1))
                    A.activation(tmpA[:, 0:DH], hl.rearrange("p m t -> p (m t)"), ACT.Square).then_inc(ybsq_done, 1)
                if p == 18:
                    a.wait_ge(ssqb_done, n(1, 1))
                    A.activation(rms[:, 3:4], pt[:, 1, 0:1], ACT.Sqrt, bias=eps[:, 0:1], scale=1.0 / DH
                                 ).then_inc(squares, 1)
                if p == 23:
                    a.wait_ge(x1_done, n(1, 1))
                    mean_root(n, 8, tmpB[:], xn[:], 4, D)
                for r in range(ROUNDS):
                    if p == Q_AT[r] + 2:
                        a.wait_ge(q_done, n(ROUNDS, r + 1))
                        if r >= 2:
                            a.wait_ge(sc_done, n(4, r - 1))
                        A.activation(qT[:, r % 2].rearrange("p q t -> p (q t)"), pt[:, r % 2], ACT.Copy
                                     ).then_inc(qT_done, 1)
                    if p == Q_AT[r] + 8:
                        a.wait_ge(best_done, n(ROUNDS, r + 1))
                        for h in range(2):
                            A.activation(gexp[:, h], best[:, h], ACT.Exp, bias=nmax[:, h:h + 1],
                                         accum_out=gsum[:, 0, h:h + 1]).then_inc(soft_done, 1)

            def gelu(s, m):
                a.wait_ge(dots, m(SLOTS, s + 1))
                a.wait_ge(diags, m(SLOTS, SLOTS + s - 7))
                A.activation(ge[:, s % 8:s % 8 + 1], zt[:, s % 8:s % 8 + 1], ACT.Gelu_apprx_tanh).then_inc(egelu, 1)

            def gelu_pair(g, m):
                gelu(2 * g, m)
                gelu(2 * g + 1, m)

            def square_y(m):
                a.wait_ge(y_taken, m(2, 3))
                A.activation(tmpA[:], tmpB[:], ACT.Square, accum_out=yrms[:, 0:1]).then_inc(y_sq, 1)
                a.wait_ge(y_sq, m(2, 1))
                A.activation(yrms[:, 1:2], yrms[:, 0:1], ACT.Sqrt, bias=eps[:, 0:1], scale=1.0 / D
                             ).then_inc(y_sq, 1)

            first = When(0)
            for p in range(STEPS):
                if p in EARLY:
                    gelu_pair(EARLY[p], first)
                front(p, first)
            with a.Fori(0, TILES - 1) as i:
                n, m = When(1, i), When(0, i)
                for g in range(LEAD, PAIRS):
                    gelu_pair(g, m)
                    front(g - LEAD, n)
                for g in range(LEAD):
                    gelu_pair(g, n)
                    if g == 0:
                        square_y(m)
            m = When(TILES - 1)
            for g in range(LEAD, PAIRS):
                gelu_pair(g, m)
            square_y(m)

        @block.tensor
        def _(t):
            T = nc.tensor

            def piece(n, k, sample):
                out, start, width, group = COLUMNS[k]
                if k == 0:
                    t.wait_ge(hT_done, n(2, 1))
                if k == 9:
                    t.wait_ge(squares, n(NORMS, 6))
                    t.wait_ge(yaT_done, n(1, 1))
                if sample:
                    t.wait_ge(first_in[k], 16)
                    w = first_place(k)
                elif k in KEPT:
                    w = wkept[:, KEPT.index(k)]
                else:
                    j = STREAMED.index(k)
                    per_tile = len(STREAMED) // 2 * 16
                    t.wait_ge(streamed_in[j % 2], n(per_tile, 16 * (j // 2 + 1) - per_tile))
                    w = wbuf[:, j % 2]
                o = start % 512
                if out:
                    for c in range(HC):
                        T.matmul(ps[group][:, o:o + width], vg[:, c * P:(c + 1) * P], w[:, c], start=c == 0,
                                 stop=c == HC - 1)
                    if k == 9:
                        t.wait_ge(ybT_done, n(1, 1))
                    for c in range(HC):
                        ins = T.matmul(ps[group + 1][:, o:o + width], xc[:, c], w[:, HC + c], start=c == 0,
                                       stop=c == HC - 1)
                elif group < 2:
                    for c in range(DC):
                        ins = T.matmul(ps[group][:, o:o + width], hT[:, c], w[:, c], start=c == 0, stop=c == DC - 1)
                else:
                    for m in range(0, width, P):
                        for c in range(DC):
                            ins = T.matmul(ps[group][:, o + m:o + m + P], w[:, c, m:m + P], hT[:, c],
                                           start=c == 0, stop=c == DC - 1)
                ins.then_inc(piece_done, 1)

            def front(p, n, sample):
                if p in (2, 25):
                    src = tmpA if p == 2 else tmpB
                    if p == 2:
                        t.wait_ge(h_done, n(1, 1))
                    else:
                        t.wait_ge(h2_done, n(1, 1))
                    if p == 2 and sample:
                        t.wait_ge(pool_set, 2)
                    for c in range(DC):
                        ins = T.transpose(pt[:, c // 4, (c % 4) * P:(c % 4 + 1) * P], src[:, c * P:(c + 1) * P],
                                          ident[:])
                    ins.then_inc(turned, 1)
                if p == 8:
                    t.wait_ge(xc_done, n(1, 1))
                    if sample:
                        t.wait_ge(wab_in, 64)
                    for j, w in enumerate((wab, wib)):
                        for m in range(HC):
                            ins = T.matmul(pt[:, j, m * P:(m + 1) * P], w[:, m], xc[:, m], start=True, stop=True)
                    ins.then_inc(gates_done, 1)
                if 4 <= p < 12:
                    if p == 4:
                        piece(n, 0, sample)
                    piece(n, p - 3, sample)
                if p == 12:
                    t.wait_ge(v_done, n(1, 1))
                    t.wait_ge(pool_set, 8 if sample else 9)
                    for g in range(GROUPS):
                        ins = T.matmul(ps[0][:, g * P:(g + 1) * P], (ws_s if sample else ws)[:, g],
                                       vg[:, g * P:(g + 1) * P], start=True, stop=True)
                    ins.then_inc(spat_done, 1)
                if p == 14:
                    t.wait_ge(ya_done, n(1, 1))
                    for c in range(HC):
                        ins = T.transpose(pt[:, 0, c * P:(c + 1) * P], ya[:, c * P:(c + 1) * P], ident[:])
                    ins.then_inc(turned, 1)
                if 18 <= p < 22:
                    piece(n, 9 + p - 18, sample)
                if p == 18:
                    t.wait_ge(ybsq_done, n(1, 1))
                    for c in range(HC):
                        ins = T.matmul(pt[:, 1, 0:1], tmpA[:, c * P:(c + 1) * P], ones[:, 0:1], start=c == 0,
                                       stop=c == HC - 1)
                    ins.then_inc(ssqb_done, 1)
                for r in range(ROUNDS):
                    if p in (Q_AT[r], Q_AT[r] + 1):
                        first = p == Q_AT[r]
                        if r == 0 and first:
                            t.wait_ge(hT_done, n(2, 2))
                        if sample and first:
                            t.wait_ge(wq_in[r], 16)
                        if r >= 2 and first:
                            t.wait_ge(qT_done, n(4, r - 1))
                        for q in (0, 1) if first else (2, 3):
                            for c in range(DC):
                                ins = T.matmul(pt[:, r % 2, q * P:(q + 1) * P],
                                               wq[:, c, (4 * r + q) * P:(4 * r + q + 1) * P], hT[:, c],
                                               start=c == 0, stop=c == DC - 1)
                        if not first:
                            ins.then_inc(q_done, 1)
                    if p == Q_AT[r] + 4:
                        t.wait_ge(qT_done, n(4, r + 1))
                        if sample and r == 0:
                            t.wait_ge(rows_in, 48)
                        for q in range(4):
                            ins = T.matmul(ps[r][:, q * P:(q + 1) * P], qT[:, r % 2, q], keys[:, q % 2], start=True,
                                           stop=True)
                        ins.then_inc(sc_done, 1)

            def weigh(s, m):
                if s == 0:
                    t.wait_ge(y_taken, m(2, 1))
                t.wait_ge(diags, m(SLOTS, SLOTS + s + 1))
                for j in range(2):
                    ins = T.matmul(accY[:, j], diag[:, s % DIAGS], ring[:, PLACE[s], D + j * 512:D + (j + 1) * 512],
                                   start=s == 0, stop=s == SLOTS - 1)
                ins.then_inc(vdone, 1)

            t.sem_inc(vdone, SLOTS)
            first = When(0)
            for p in range(STEPS):
                if p in EARLY:
                    weigh(2 * EARLY[p], first)
                front(p, first, True)
                if p in EARLY:
                    weigh(2 * EARLY[p] + 1, first)
            with t.Fori(0, TILES - 1) as i:
                n, m = When(1, i), When(0, i)
                for g in range(LEAD, PAIRS):
                    weigh(2 * g, m)
                    front(g - LEAD, n, False)
                    weigh(2 * g + 1, m)
                for s in range(2 * LEAD):
                    weigh(s, n)
            m = When(TILES - 1)
            for s in range(2 * LEAD, SLOTS):
                weigh(s, m)


def kernel(**inputs):
    import numpy as np
    import concourse.bacc as bacc
    from concourse.bass_utils import run_bass_kernel_spmd

    a = {k: np.asarray(x) for k, x in inputs.items()}

    def by_channel(x):
        x = x.reshape(x.shape[:-1] + (x.shape[-1] // P, P))
        return np.moveaxis(x, (-1, -2), (0, 1)).reshape(P, -1)

    bs = a["b_s"][0].T
    cols = np.concatenate([
        by_channel(a["g_mix"][0]), by_channel(a["g_out_a"][0]), by_channel(a["g_out_b"][0]),
        by_channel(a["conv_w"][0]), by_channel(a["conv_b"][0]), by_channel(a["b_a"][0]), by_channel(a["b_i"][0]),
        by_channel(a["lam"][0]), bs, np.concatenate([bs[0:NT]] * NB, axis=0)], axis=1)
    feed = {
        "x_all": np.concatenate([a["x_sample"].reshape(NB * NT, D), a["x_prompt"].reshape(-1, D)], axis=0),
        "cols": cols,
        "conv_state": by_channel(a["state_conv"][0]).reshape(P, HC, NB, HIST),
        "lru_state": by_channel(a["state_lru"][0]).reshape(P, HC, NB),
        "w_in": a["w_in"][0], "w_out": a["w_out"][0], "w_q": a["w_q"][0],
        "ws_t": np.transpose(a["w_s"][0], (2, 0, 1)),
        "w_a": a["w_a"][0], "w_i": a["w_i"][0],
        "keys_t": np.stack([a["k_sub1"][0].T, a["k_sub2"][0].T], axis=1),
        "rows": np.concatenate([a["g_ffn"][0], a["g_final"], a["g_v"][0]])[None, :],
        "experts": np.concatenate([a["u_tab"][0], a["v_tab"][0]], axis=1),
    }
    feed = {k: np.ascontiguousarray(x) for k, x in feed.items()}
    nc = bacc.Bacc("TRN2", target_bir_lowering=False, num_devices=1)
    args = [nc.dram_tensor(k, x.shape, mybir.dt.from_np(x.dtype), kind="ExternalInput").ap() for k, x in feed.items()]
    outs = {"y_all": (TILES * P, D), "v_rows": (P, DH), "state_sample": (P, HC * NB * (HIST + 1)),
            "state_prompt": (P, HC * NB * (HIST + 1))}
    args += [nc.dram_tensor(k, s, F32, kind="ExternalOutput").ap() for k, s in outs.items()]
    hybrid_layer(nc, *args)
    got = run_bass_kernel_spmd(nc, [feed], core_ids=[0]).results[0]
    y = got["y_all"]
    ss = got["state_sample"].reshape(P, HC, NB * (HIST + 1))
    sp = got["state_prompt"].reshape(P, HC, NB * (HIST + 1))

    def channels(x):
        x = np.moveaxis(x, (1, 0), (-2, -1))
        return np.ascontiguousarray(x.reshape(x.shape[:-2] + (DH,)))

    conv_s = channels(ss[:, :, 0:NB * HIST].reshape(P, HC, NB, HIST))[None]
    lru_s = channels(ss[:, :, NB * HIST:])[None]
    conv_p = channels(sp[:, :, 0:HIST])[None, None]
    lru_p = channels(sp[:, :, HIST])[None, None]
    return (y[P:].reshape(1, -1, D), y[0:P].reshape(NB, NT, D), conv_p, lru_p, conv_s, lru_s,
            got["v_rows"].reshape(1, NB, NT, DH))
```
